# Optimizing a Trainium2 kernel written in Bass

```python
import jax, jax.numpy as jnp
from jax import lax
import numpy as np
import math

D_MODEL = 1024
BATCH = 1
SEQ = 256
DEPTH = 2

HEAD_DIM = 64
POOL_WIDTH = D_MODEL // 4
POOL_WINDOWS = (2, 4, 8, 16)
N_POOL_GROUPS = len(POOL_WINDOWS)
POOL_GROUP_DIM = POOL_WIDTH // N_POOL_GROUPS
CONV_WIDTH = (3 * D_MODEL) // 8
CONV_KERNEL = 31
SGU_WIDTH = D_MODEL - POOL_WIDTH - CONV_WIDTH
SGU_HEADS = SGU_WIDTH // HEAD_DIM
CHUNK = 128
D_MIX = POOL_WIDTH + CONV_WIDTH + SGU_WIDTH
D_IN = POOL_WIDTH + 2 * CONV_WIDTH + 2 * SGU_WIDTH
D_FF = ((8 * D_MODEL // 3 + 127) // 128) * 128
N_EXPERTS = 8
TOP_K = 2
D_FF_EXPERT = 7 * D_MODEL // 2
N_MOD = 6
EPS = 1e-6


def rms_norm(x, g):
    xf = x.astype(jnp.float32)
    y = xf * lax.rsqrt(jnp.mean(xf * xf, axis=-1, keepdims=True) + EPS)
    return (y * g.astype(jnp.float32)).astype(x.dtype)

def layer_norm(x, g, b):
    xf = x.astype(jnp.float32)
    mu = jnp.mean(xf, axis=-1, keepdims=True)
    var = jnp.mean(jnp.square(xf - mu), axis=-1, keepdims=True)
    y = (xf - mu) * lax.rsqrt(var + EPS) * g.astype(jnp.float32) + b.astype(jnp.float32)
    return y.astype(x.dtype)

def multiscale_pool(a, pool_w, pool_scale):
    S = a.shape[1]
    af = a.astype(jnp.float32)
    cs = jnp.pad(jnp.cumsum(af, axis=1), ((0, 0), (1, 0), (0, 0)))
    t = jnp.arange(S)
    outs = []
    for g, w in enumerate(POOL_WINDOWS):
        half = w // 2
        hi = jnp.clip(t + half, 0, S)
        lo = jnp.clip(t - half, 0, S)
        sl = slice(g * POOL_GROUP_DIM, (g + 1) * POOL_GROUP_DIM)
        cs_g = cs[:, :, sl]
        win_sum = jnp.take(cs_g, hi, axis=1) - jnp.take(cs_g, lo, axis=1)
        count = (hi - lo).astype(jnp.float32)[None, :, None]
        diff = (win_sum / count - af[:, :, sl]).astype(a.dtype)
        outs.append(jnp.einsum('bsc,cd->bsd', diff, pool_w[g]))
    return jnp.concatenate(outs, axis=-1) * pool_scale

def conformer_conv(p, conv_w, conv_b, ln_g, ln_b):
    val, gate = jnp.split(p, 2, axis=-1)
    glu = val * jax.nn.sigmoid(gate)
    y = lax.conv_general_dilated(
        glu, conv_w[:, None, :], window_strides=(1,),
        padding=[(CONV_KERNEL // 2, CONV_KERNEL // 2)],
        dimension_numbers=('NWC', 'WIO', 'NWC'),
        feature_group_count=CONV_WIDTH) + conv_b
    return jax.nn.silu(layer_norm(y, ln_g, ln_b))

def spatial_gating(p, ln_g, ln_b, sgu_w, sgu_b):
    B, S, _ = p.shape
    u, v = jnp.split(p, 2, axis=-1)
    v = layer_norm(v, ln_g, ln_b).reshape(B, S // CHUNK, CHUNK, SGU_HEADS, HEAD_DIM)
    mixed = jnp.einsum('hpq,bnqhd->bnphd', sgu_w, v) + sgu_b.T[:, :, None]
    return u * mixed.reshape(B, S, SGU_WIDTH)

def swiglu(h, w_gate, w_up, w_down):
    return (jax.nn.silu(h @ w_gate) * (h @ w_up)) @ w_down

def moe_swiglu(h, router_w, router_b, w_gate, w_up, w_down):
    logits = jnp.einsum('bsd,de->bse', h.astype(jnp.float32), router_w.astype(jnp.float32)) \
        + router_b.astype(jnp.float32)
    top_vals, top_idx = lax.top_k(logits, TOP_K)
    top_w = jax.nn.softmax(top_vals, axis=-1)
    combine = jnp.sum(jax.nn.one_hot(top_idx, N_EXPERTS, dtype=jnp.float32) * top_w[..., None], axis=-2)
    combine = combine.astype(h.dtype)
    y = jnp.zeros_like(h)
    for e in range(N_EXPERTS):
        y = y + combine[..., e:e + 1] * swiglu(h, w_gate[e], w_up[e], w_down[e])
    return y

def first_inputs(seed: int = 0) -> dict:
    key = jax.random.key(seed)
    ks = jax.random.split(key, 32)
    n_dense = (DEPTH + 1) // 2
    n_moe = DEPTH // 2

    def nrm(k, shape, fan_in):
        return jax.random.normal(k, shape, jnp.float32) * (fan_in ** -0.5)

    def near_one(k, shape):
        return 1.0 + 0.1 * jax.random.normal(k, shape, jnp.float32)

    def small(k, shape):
        return 0.02 * jax.random.normal(k, shape, jnp.float32)

    return {
        "x": jax.random.normal(ks[0], (BATCH, SEQ, D_MODEL), jnp.float32),
        "c": jax.random.normal(ks[1], (BATCH, D_MODEL), jnp.float32),
        "ada_w": nrm(ks[2], (DEPTH, D_MODEL, N_MOD * D_MODEL), D_MODEL),
        "ada_b": small(ks[3], (DEPTH, N_MOD * D_MODEL)),
        "mix_norm_g": near_one(ks[4], (DEPTH, D_MODEL)),
        "ffn_norm_g": near_one(ks[5], (DEPTH, D_MODEL)),
        "w_in": nrm(ks[6], (DEPTH, D_MODEL, D_IN), D_MODEL),
        "pool_w": nrm(ks[7], (DEPTH, N_POOL_GROUPS, POOL_GROUP_DIM, POOL_GROUP_DIM), POOL_GROUP_DIM),
        "pool_scale": near_one(ks[8], (DEPTH, POOL_WIDTH)),
        "conv_w": nrm(ks[9], (DEPTH, CONV_KERNEL, CONV_WIDTH), CONV_KERNEL),
        "conv_b": small(ks[10], (DEPTH, CONV_WIDTH)),
        "conv_ln_g": near_one(ks[11], (DEPTH, CONV_WIDTH)),
        "conv_ln_b": small(ks[12], (DEPTH, CONV_WIDTH)),
        "sgu_ln_g": near_one(ks[13], (DEPTH, SGU_WIDTH)),
        "sgu_ln_b": small(ks[14], (DEPTH, SGU_WIDTH)),
        "sgu_w": nrm(ks[15], (DEPTH, SGU_HEADS, CHUNK, CHUNK), CHUNK),
        "sgu_b": near_one(ks[16], (DEPTH, SGU_HEADS, CHUNK)),
        "w_out": nrm(ks[17], (DEPTH, D_MIX, D_MODEL), D_MIX),
        "ffn_w_gate": nrm(ks[18], (n_dense, D_MODEL, D_FF), D_MODEL),
        "ffn_w_up": nrm(ks[19], (n_dense, D_MODEL, D_FF), D_MODEL),
        "ffn_w_down": nrm(ks[20], (n_dense, D_FF, D_MODEL), D_FF),
        "router_w": nrm(ks[21], (n_moe, D_MODEL, N_EXPERTS), D_MODEL),
        "router_b": 0.01 * jax.random.normal(ks[22], (n_moe, N_EXPERTS), jnp.float32),
        "moe_w_gate": nrm(ks[23], (n_moe, N_EXPERTS, D_MODEL, D_FF_EXPERT), D_MODEL),
        "moe_w_up": nrm(ks[24], (n_moe, N_EXPERTS, D_MODEL, D_FF_EXPERT), D_MODEL),
        "moe_w_down": nrm(ks[25], (n_moe, N_EXPERTS, D_FF_EXPERT, D_MODEL), D_FF_EXPERT),
        "final_norm_g": near_one(ks[26], (D_MODEL,)),
    }

def first_block(x, c, ada_w, ada_b, mix_norm_g, ffn_norm_g, w_in, pool_w, pool_scale,
              conv_w, conv_b, conv_ln_g, conv_ln_b, sgu_ln_g, sgu_ln_b, sgu_w, sgu_b, w_out,
              ffn_w_gate, ffn_w_up, ffn_w_down, router_w, router_b,
              moe_w_gate, moe_w_up, moe_w_down, final_norm_g):
    cond = jax.nn.silu(c)
    for l in range(DEPTH):
        mod = cond @ ada_w[l] + ada_b[l]
        mods = jnp.split(mod[:, None, :], N_MOD, axis=-1)
        shift_m, scale_m, gate_m, shift_f, scale_f, gate_f = mods

        h = rms_norm(x, mix_norm_g[l]) * (1.0 + scale_m) + shift_m
        proj = h @ w_in[l]
        p_pool, p_conv, p_sgu = jnp.split(proj, [POOL_WIDTH, POOL_WIDTH + 2 * CONV_WIDTH], axis=-1)
        out_a = multiscale_pool(p_pool, pool_w[l], pool_scale[l])
        out_b = conformer_conv(p_conv, conv_w[l], conv_b[l], conv_ln_g[l], conv_ln_b[l])
        out_c = spatial_gating(p_sgu, sgu_ln_g[l], sgu_ln_b[l], sgu_w[l], sgu_b[l])
        mixed = jnp.concatenate([out_a, out_b, out_c], axis=-1)
        x = x + gate_m * (mixed @ w_out[l])

        h = rms_norm(x, ffn_norm_g[l]) * (1.0 + scale_f) + shift_f
        i = l // 2
        if l % 2 == 0:
            y = swiglu(h, ffn_w_gate[i], ffn_w_up[i], ffn_w_down[i])
        else:
            y = moe_swiglu(h, router_w[i], router_b[i], moe_w_gate[i], moe_w_up[i], moe_w_down[i])
        x = x + gate_f * y
    return rms_norm(x, final_norm_g)


CTX_LEN = 256
GRID_W = 64
HG_WIDTH = D_MODEL // 2
HG_DIM = 128
HG_HEADS = HG_WIDTH // HG_DIM
CHUNK_2 = 64
DA_WIDTH = D_MODEL // 4
DA_HEADS = 4
DA_V = DA_WIDTH // DA_HEADS
DA_QK = DA_V // 2
DA_QK_WIDTH = DA_HEADS * 2 * DA_QK
Q_BLOCK = 128
ROPE_THETA = 10000.0
ROPE_AXIS_DIM = DA_QK // 2
FT_WIDTH = D_MODEL // 4
FT_GROUPS = 4
MIX_WIDTH = HG_WIDTH + DA_WIDTH + FT_WIDTH
IN_SPLITS = (HG_WIDTH, HG_WIDTH, HG_WIDTH, HG_WIDTH, HG_WIDTH, DA_QK_WIDTH, DA_QK_WIDTH, DA_WIDTH, FT_WIDTH)
IN_WIDTH = sum(IN_SPLITS)
FF_HIDDEN = ((8 * D_MODEL // 3 + 255) // 256) * 256


def rms_norm_2(x, g):
    xf = x.astype(jnp.float32)
    y = xf * lax.rsqrt(jnp.mean(xf * xf, axis=-1, keepdims=True) + EPS)
    return (y * g.astype(jnp.float32)).astype(x.dtype)

def adaln(x, g, shift, scale):
    return rms_norm_2(x, g) * (1 + scale) + shift

def modulation(cond, w, b):
    return jnp.split(jax.nn.silu(cond) @ w + b, N_MOD, axis=-1)

def split_heads(a, h):
    return a.reshape(a.shape[:-1] + (h, a.shape[-1] // h))

def split_projection(p):
    offsets = [int(o) for o in np.cumsum(IN_SPLITS)[:-1]]
    return jnp.split(p, offsets, axis=-1)

def axial_rope(t_len):
    n_rows = t_len // GRID_W
    rows = jnp.broadcast_to(jnp.arange(n_rows)[:, None], (n_rows, GRID_W)).reshape(-1)
    cols = jnp.broadcast_to(jnp.arange(GRID_W)[None, :], (n_rows, GRID_W)).reshape(-1)
    inv_freq = 1.0 / (ROPE_THETA ** (jnp.arange(0, ROPE_AXIS_DIM, 2, dtype=jnp.float32) / ROPE_AXIS_DIM))
    ang = jnp.stack([rows, cols], axis=-1).astype(jnp.float32)[:, :, None] * inv_freq
    return jnp.cos(ang), jnp.sin(ang)

def apply_rope(x, cos, sin):
    xs = x.reshape(x.shape[:-1] + (2, 2, ROPE_AXIS_DIM // 2)).astype(jnp.float32)
    cs, sn = cos[None, :, None, None], sin[None, :, None, None]
    x1, x2 = xs[..., 0, :], xs[..., 1, :]
    out = jnp.stack([x1 * cs - x2 * sn, x2 * cs + x1 * sn], axis=-2)
    return out.reshape(x.shape).astype(x.dtype)

def gla_chunkwise(q, k, v, log_f, s0):
    b_, t_, h_, _ = q.shape
    dv = v.shape[-1]
    n = t_ // CHUNK_2

    def chunks(a):
        return a.astype(jnp.float32).reshape(b_, n, CHUNK_2, h_, a.shape[-1]).transpose(1, 0, 3, 2, 4)

    incl = jnp.tril(jnp.ones((CHUNK_2, CHUNK_2), dtype=bool))[:, :, None]

    def step(state, inp):
        qi, ki, vi, gi = inp
        bcum = jnp.cumsum(gi, axis=2)
        o_inter = jnp.einsum('bhtk,bhkv->bhtv', qi * jnp.exp(bcum), state)
        rel = bcum[:, :, :, None, :] - bcum[:, :, None, :, :]
        decay = jnp.exp(jnp.where(incl, rel, -jnp.inf))
        scores = jnp.einsum('bhtk,bhsk,bhtsk->bhts', qi, ki, decay)
        o_intra = jnp.einsum('bhts,bhsv->bhtv', scores, vi)
        blast = bcum[:, :, -1:, :]
        state = state * jnp.exp(blast[:, :, 0, :, None]) + jnp.einsum(
            'bhsk,bhsv->bhkv', ki * jnp.exp(blast - bcum), vi)
        return state, o_inter + o_intra

    s_fin, o = lax.scan(step, s0, (chunks(q), chunks(k), chunks(v), chunks(log_f)))
    return o.transpose(1, 0, 3, 2, 4).reshape(b_, t_, h_, dv), s_fin

def hgrn2_scan(q, v, z, lb, s0, reverse):
    f = lb + (1.0 - lb) * jax.nn.sigmoid(z.astype(jnp.float32))
    k = split_heads(1.0 - f, HG_HEADS)
    log_f = split_heads(jnp.log(f), HG_HEADS)
    if reverse:
        q, k, v, log_f = jnp.flip(q, 1), jnp.flip(k, 1), jnp.flip(v, 1), jnp.flip(log_f, 1)
    o, s = gla_chunkwise(q, k, v, log_f, s0)
    if reverse:
        o = jnp.flip(o, 1)
    return o, s

def diff_softmax_attend(q, keys, vals, lam):
    s = jnp.einsum('bqhmd,bkhmd->bhmqk', q, keys).astype(jnp.float32) * (DA_QK ** -0.5)
    p = jax.nn.softmax(s, axis=-1)
    w = p[:, :, 0] - lam * p[:, :, 1]
    return jnp.einsum('bhqk,bkhv->bqhv', w.astype(vals.dtype), vals)

def fourier_mix(u):
    uh = split_heads(u, FT_GROUPS).astype(jnp.float32)
    y = jnp.fft.fft2(uh, axes=(1, 3), norm="ortho").real
    return y.reshape(u.shape).astype(u.dtype)

def mixer(hl, hc, w_in, w_out, lb_f, lb_b, hg_onorm, da_lam, da_subln, lam_init, cos, sin, with_ctx):
    pl = split_projection(hl @ w_in)
    pc = split_projection(hc @ w_in)
    bsz, t_lat = hl.shape[0], hl.shape[1]

    s0 = jnp.zeros((bsz, HG_HEADS, HG_DIM, HG_DIM), jnp.float32)
    q_c, v_c = split_heads(jax.nn.silu(pc[0]), HG_HEADS), split_heads(pc[1], HG_HEADS)
    q_l, v_l = split_heads(jax.nn.silu(pl[0]), HG_HEADS), split_heads(pl[1], HG_HEADS)
    oc_f, st_f = hgrn2_scan(q_c, v_c, pc[3], lb_f, s0, False)
    oc_b, st_b = hgrn2_scan(q_c, v_c, pc[4], lb_b, s0, True)
    ol_f, _ = hgrn2_scan(q_l, v_l, pl[3], lb_f, st_f, False)
    ol_b, _ = hgrn2_scan(q_l, v_l, pl[4], lb_b, st_b, True)

    def hgrn_out(o, g):
        return (rms_norm_2(o, hg_onorm).reshape(g.shape) * jax.nn.silu(g)).astype(g.dtype)

    def qk_heads(a):
        return a.reshape(a.shape[:-1] + (DA_HEADS, 2, DA_QK))

    lam_f = da_lam.astype(jnp.float32)
    lam = jnp.exp(jnp.sum(lam_f[0] * lam_f[1])) - jnp.exp(jnp.sum(lam_f[2] * lam_f[3])) + lam_init
    dq_l, dk_l = apply_rope(qk_heads(pl[5]), cos, sin), apply_rope(qk_heads(pl[6]), cos, sin)
    dv_l = split_heads(pl[7], DA_HEADS)
    dq_c, dk_c, dv_c = qk_heads(pc[5]), qk_heads(pc[6]), split_heads(pc[7], DA_HEADS)
    keys = jnp.concatenate([dk_l, dk_c], axis=1)
    vals = jnp.concatenate([dv_l, dv_c], axis=1)
    nb = t_lat // Q_BLOCK
    qb = dq_l.reshape((bsz, nb, Q_BLOCK) + dq_l.shape[2:]).transpose(1, 0, 2, 3, 4, 5)
    od_l = lax.map(lambda qq: diff_softmax_attend(qq, keys, vals, lam), qb)
    od_l = od_l.transpose(1, 0, 2, 3, 4).reshape(bsz, t_lat, DA_HEADS, DA_V)

    def diff_out(o):
        return (rms_norm_2(o, da_subln) * (1.0 - lam_init)).reshape(o.shape[:2] + (DA_WIDTH,))

    yl = jnp.concatenate([hgrn_out(ol_f + ol_b, pl[2]), diff_out(od_l).astype(hl.dtype),
                          fourier_mix(pl[8])], axis=-1) @ w_out
    if not with_ctx:
        return yl, None
    od_c = diff_softmax_attend(dq_c, dk_c, dv_c, lam)
    yc = jnp.concatenate([hgrn_out(oc_f + oc_b, pc[2]), diff_out(od_c).astype(hc.dtype),
                          fourier_mix(pc[8])], axis=-1) @ w_out
    return yl, yc

def swiglu_2(h, w_i, w_o):
    g, u = jnp.split(h @ w_i, 2, axis=-1)
    return (jax.nn.silu(g) * u) @ w_o

def second_inputs(seed: int = 0) -> dict:
    key = jax.random.key(seed)
    ks = jax.random.split(key, 15)
    f32 = jnp.float32
    nrm = lambda k, s: jax.random.normal(k, s, f32)
    return {
        "x": nrm(ks[0], (BATCH, SEQ, D_MODEL)),
        "c": nrm(ks[1], (BATCH, D_MODEL)),
        "ctx": nrm(ks[2], (BATCH, CTX_LEN, D_MODEL)),
        "c_ctx": nrm(ks[3], (D_MODEL,)),
        "w_mod": nrm(ks[4], (DEPTH, D_MODEL, N_MOD * D_MODEL)) * (0.5 * D_MODEL ** -0.5),
        "b_mod": nrm(ks[5], (DEPTH, N_MOD * D_MODEL)) * 0.01,
        "norm_g": 1.0 + 0.02 * nrm(ks[6], (DEPTH, 4, D_MODEL)),
        "w_in": nrm(ks[7], (DEPTH, D_MODEL, IN_WIDTH)) * D_MODEL ** -0.5,
        "w_out": nrm(ks[8], (DEPTH, MIX_WIDTH, D_MODEL)) * MIX_WIDTH ** -0.5,
        "hg_lb_logits": 0.1 * nrm(ks[9], (2, DEPTH, HG_WIDTH)),
        "hg_onorm": 1.0 + 0.02 * nrm(ks[10], (DEPTH, HG_DIM)),
        "da_lambda": 0.1 * nrm(ks[11], (DEPTH, 4, DA_QK)),
        "da_subln": 1.0 + 0.02 * nrm(ks[12], (DEPTH, DA_V)),
        "w_ffn_in": nrm(ks[13], (DEPTH, D_MODEL, 2 * FF_HIDDEN)) * D_MODEL ** -0.5,
        "w_ffn_out": nrm(ks[14], (DEPTH, FF_HIDDEN, D_MODEL)) * FF_HIDDEN ** -0.5,
    }

def second_block(x, c, ctx, c_ctx, w_mod, b_mod, norm_g, w_in, w_out, hg_lb_logits, hg_onorm,
              da_lambda, da_subln, w_ffn_in, w_ffn_out):
    cos, sin = axial_rope(x.shape[1])
    lb_p = jax.nn.softmax(hg_lb_logits.astype(jnp.float32), axis=1)
    lower_bounds = jnp.cumsum(lb_p, axis=1) - lb_p[:, :1]
    xl, xc = x, ctx
    for l in range(DEPTH):
        with_ctx = l < DEPTH - 1
        lam_init = 0.8 - 0.6 * math.exp(-0.3 * l)
        ml = modulation(c[:, None, :], w_mod[l], b_mod[l])
        mc = modulation(c_ctx[None, None, :], w_mod[l], b_mod[l])
        g = norm_g[l]
        hl = adaln(xl, g[0], ml[0], ml[1])
        hc = adaln(xc, g[0], mc[0], mc[1])
        yl, yc = mixer(hl, hc, w_in[l], w_out[l], lower_bounds[0, l], lower_bounds[1, l], hg_onorm[l],
                       da_lambda[l], da_subln[l], lam_init, cos, sin, with_ctx)
        xl = xl + ml[2] * rms_norm_2(yl, g[1])
        xl = xl + ml[5] * rms_norm_2(swiglu_2(adaln(xl, g[2], ml[3], ml[4]), w_ffn_in[l], w_ffn_out[l]), g[3])
        if with_ctx:
            xc = xc + mc[2] * rms_norm_2(yc, g[1])
            xc = xc + mc[5] * rms_norm_2(swiglu_2(adaln(xc, g[2], mc[3], mc[4]), w_ffn_in[l], w_ffn_out[l]), g[3])
    return xl


def setup_inputs(seed=0):
    out = dict(first_inputs(seed))
    for name, value in second_inputs(seed + 1).items():
        if name != "x":
            out[name + "_2"] = value
    return out


def reference(
    x, c, ada_w, ada_b, mix_norm_g, ffn_norm_g, w_in, pool_w, pool_scale, conv_w, conv_b,
    conv_ln_g, conv_ln_b, sgu_ln_g, sgu_ln_b, sgu_w, sgu_b, w_out, ffn_w_gate, ffn_w_up,
    ffn_w_down, router_w, router_b, moe_w_gate, moe_w_up, moe_w_down, final_norm_g, c_2, ctx_2,
    c_ctx_2, w_mod_2, b_mod_2, norm_g_2, w_in_2, w_out_2, hg_lb_logits_2, hg_onorm_2,
    da_lambda_2, da_subln_2, w_ffn_in_2, w_ffn_out_2,
):
    x = first_block(
        x, c, ada_w, ada_b, mix_norm_g, ffn_norm_g, w_in, pool_w, pool_scale, conv_w, conv_b,
        conv_ln_g, conv_ln_b, sgu_ln_g, sgu_ln_b, sgu_w, sgu_b, w_out, ffn_w_gate, ffn_w_up,
        ffn_w_down, router_w, router_b, moe_w_gate, moe_w_up, moe_w_down, final_norm_g,
    )
    return second_block(
        x, c_2, ctx_2, c_ctx_2, w_mod_2, b_mod_2, norm_g_2, w_in_2, w_out_2, hg_lb_logits_2,
        hg_onorm_2, da_lambda_2, da_subln_2, w_ffn_in_2, w_ffn_out_2,
    )


_drawn_inputs = setup_inputs


def setup_inputs(seed=0):
    import zlib

    import numpy as np

    out = dict(_drawn_inputs(seed))
    spreads = {}
    factors = {'conv_b': 5.903,
     'conv_ln_b': 4.011,
     'router_b': 4.011,
     'norm_g_2': 3.037,
     'hg_lb_logits_2': 8.0,
     'hg_onorm_2': 8.0,
     'da_subln_2': 8.0}
    for name, (base, spread) in spreads.items():
        noise = np.random.default_rng([zlib.crc32(name.encode()), seed]).standard_normal(out[name].shape)
        drawn = base * np.exp(spread * noise) if base else spread * noise
        out[name] = __import__('jax').numpy.asarray(drawn.astype(out[name].dtype))
    for name, factor in factors.items():
        out[name] = (out[name] * factor).astype(out[name].dtype)
    return out
```

```python
import math
from contextlib import ExitStack

import numpy as np

import concourse.bass as bass
from concourse import mybir

ALU = mybir.AluOpType
ACT = mybir.ActivationFunctionType
F32 = mybir.dt.float32
U8 = mybir.dt.uint8
I32 = mybir.dt.int32
AX_X = mybir.AxisListType.X

P = 128
D = 1024
KC = D // P
SEQ = 256
TX = SEQ // P
POOL_W, CONV_W, SGU_W = 256, 384, 384
CC = CONV_W // P
TAPS = 31
PAD = TAPS // 2
SGU_HEADS = 6
N_MOD = 6
MODC = N_MOD * KC
FF = 2816
FFC = FF // P
GU = 256
E_ = 8
FFE = 3584
EPS = 1e-6
SLOTS = 4
HG = 512
HEADS = 4
LEVELS = 7
LN_FLOOR = 2.0 ** -63
LAM_INIT = [0.8 - 0.6 * math.exp(-0.3 * l) for l in range(2)]
ATT_SCALE = 32 ** -0.5
POOL_WINDOWS = (2, 4, 8, 16)


class Count:

    def __init__(self):
        self.n, self.k, self.per, self.it = {}, {}, {}, None

    def up(self, sem, by=1):
        s = id(sem)
        if self.it is None:
            self.n[s] = self.n.get(s, 0) + by
            return self.n[s]
        assert s in self.per, sem
        self.k[s] = self.k.get(s, 0) + by
        return self.it * self.per[s] + (self.n.get(s, 0) + self.k[s])

    def at(self, sem):
        s = id(sem)
        now = self.n.get(s, 0) + self.k.get(s, 0)
        return now if self.it is None else self.it * self.per[s] + now

    def begin(self, it, *per):
        self.it, self.per, self.k = it, {id(s): n for s, n in per}, {}

    def end(self, passes):
        for s, n in self.per.items():
            assert self.k.get(s, 0) == n, (self.k.get(s, 0), n)
            self.n[s] = self.n.get(s, 0) + n * passes
        self.it, self.per, self.k = None, {}, {}


MOD_BLOCKS = {0: 12, 1: 4, 2: 4, 3: 0}
NARROW = 256
NARROW_TAIL = {0: 4, 1: 0, 2: 4, 3: 0}
NARROW_ALL = N_MOD * D // NARROW


def narrow_first(M):
    return MOD_BLOCKS[M] * 512 // NARROW


def narrow_plan(units, blocks):
    done = [2 * blocks * (u + 1) // (units - 1) for u in range(units - 1)]
    return [b - a for a, b in zip([0] + done, done)] + [0]


def narrow_ends(units, blocks):
    out, n = [], 0
    for k in narrow_plan(units, blocks):
        out.append([h // 2 for h in range(n, n + k) if h % 2])
        n += k
    return out


MOE_ORDER = [("gu", 0), ("gu", 1), ("gu", 2), ("gu", 3)]
for _j in range(5):
    MOE_ORDER += [("down", _j), ("gu", 2 * _j + 4), ("gu", 2 * _j + 5)]
MOE_ORDER += [("down", 5), ("down", 6)]


def shape_constants():
    i = np.arange(P)
    ident = np.eye(P, dtype=np.float32)
    tri = np.stack([i[:, None] <= i[None], i[:, None] >= i[None], i[:, None] > i[None], i[:, None] < i[None]], 1)
    masks = np.zeros((P, 2, LEVELS, P), np.uint8)
    for lv in range(LEVELS):
        m = P >> (lv + 1)
        left = (i // m) % 2 == 0
        same = (i[:, None] // (2 * m)) == (i[None] // (2 * m))
        masks[:, 0, lv] = same & left[:, None] & ~left[None]
        masks[:, 1, lv] = same & ~left[:, None] & left[None]
    band = np.zeros((SEQ, 4, SEQ), np.float32)
    for g, w in enumerate(POOL_WINDOWS):
        for t in range(SEQ):
            lo, hi = max(t - w // 2, 0), min(t + w // 2, SEQ)
            band[lo:hi, g, t] = np.float32(1) / np.float32(hi - lo)
            band[t, g, t] -= 1
    n = np.arange(SEQ)
    ang = 2 * np.pi * ((n[:, None] * n[None]) % SEQ) / SEQ
    dft_tok = np.concatenate([np.cos(ang), np.sin(ang)], 1) / np.sqrt(SEQ)
    c = np.arange(64)
    angc = 2 * np.pi * ((c[:, None] * c[None]) % 64) / 64
    dft_ch = np.zeros((P, 2, P))
    for h in range(2):
        dft_ch[64 * h:64 * h + 64, 0, 64 * h:64 * h + 64] = np.cos(angc) / 8
        dft_ch[64 * h:64 * h + 64, 1, 64 * h:64 * h + 64] = -np.sin(angc) / 8
    inv = 1.0 / (10000.0 ** (np.arange(0, 16, 2, dtype=np.float32) / np.float32(16)))
    pos = np.stack([n // 64, n % 64], -1).astype(np.float32)[:, :, None] * inv.astype(np.float32)
    cos, sin = np.cos(pos), np.sin(pos)
    rope = np.stack([np.stack([cos, cos], 2), np.stack([-sin, sin], 2)], 1).reshape(SEQ, 2, 32)
    f = lambda a: np.ascontiguousarray(a, dtype=np.float32)
    return {
        "k_ident": ident, "k_tri": f(tri), "k_masks": masks.reshape(P, -1).view(np.int32),
         "k_band": band,
        "k_dft_tok": f(dft_tok), "k_dft_ch": f(dft_ch), "k_rope": f(rope),
        "k_iota": f(np.tile(np.arange(2 * P), (P, 1))),
    }


def program(nc, a, out, stages):
    ctx = ExitStack()
    with ctx:
        def sb(name, shape, dt=F32):
            return ctx.enter_context(nc.sbuf_tensor("sb_" + name, shape, dt))

        def sem(name):
            return ctx.enter_context(nc.semaphore(name))

        ring = [sb(f"weights{j}", [P, KC, 512]) for j in range(SLOTS)]
        x = sb("x", [P, 4, D])
        hT = sb("hT", [P, KC, 512])
        mixT = sb("mixT", [P, KC, 512])
        xn = sb("xn", [P, 2, D])
        gate_bc = sb("gate_bc", [P, 2, D])
        ident = sb("ident", [P, P])
        ones = sb("ones", [P, P])
        tri = sb("tri", [P, 4, P])
        mask_words = sb("mask_words", [P, 2 * LEVELS * P // 4], I32)
        masks = mask_words[:, :].bitcast(U8).rearrange("p (d l t) -> p d l t", d=2, l=LEVELS)
        cols = sb("cols", [P, 310])
        conv_cols = sb("conv_cols", [P, 2 * CC, TAPS])
        cond_raw = sb("cond_raw", [P, 3, KC])
        cond = sb("cond", [P, KC, 3])
        mod_sum = sb("mod_sum", [P, 2, 2, NARROW])
        rows = mod_sum[0:3].rearrange("p b s n -> p b (s n)")
        modcol = sb("modcol", [P, 2, MODC, 3])
        acol = sb("acol", [P, 2, 2, KC])
        gcol = sb("gcol", [P, 2, 2, KC])
        rope = sb("rope", [P, TX, 2, 32])
        st = sb("stats", [P, 64])
        eps = sb("eps", [P, 1])
        free_marks = sb("free_marks", [1, 16])
        arena = sb("arena", [P, 16384])

        def view(off, *shape):
            n = int(np.prod(shape))
            names = "abcd"[:len(shape)]
            v = arena[:, off:off + n]
            if len(shape) > 1:
                v = v.rearrange(f"p ({' '.join(names)}) -> p {' '.join(names)}",
                                **{c: s for c, s in zip(names[1:], shape[1:])})
            return v

        PARAMS = 9216
        packs = view(PARAMS - 1024, 8, P)
        band = view(PARAMS, TX, 4 * SEQ)
        sgu_raw = view(PARAMS + 2048, 2 * SGU_HEADS, P)
        sgu_bias = view(PARAMS + 3584, 2 * SGU_HEADS * P)
        pool_bd = view(PARAMS + 5120, 4, P)
        sgu_ln = view(PARAMS + 5632, 4, SGU_W)
        glu = view(0, CC, SEQ + 2 * PAD)
        sig = view(860, CC, SEQ)
        conv_y = view(1628, CC, SEQ)
        conv_sq = view(2396, CC, SEQ)
        pool_tok = view(3164, TX, POOL_W)
        diffT = view(3676, 2, SEQ)
        v_n = view(4188, TX, SGU_W)
        uT = view(4956, CC, SEQ)
        sgu_wT = view(5724, SGU_HEADS, P)
        lnw = view(6492, 2, SEQ)
        prod = view(7004, 512)
        conv_raw = view(PARAMS - 1024 - 768, 2 * CC * P)

        def ff_space(T):
            n = FFC * T * P
            return view(0, FFC, T * P), view(n, 2, GU), view(n + 512, 2, GU)

        ybuf = view(12288, 4, D)
        diag1 = view(7552, KC, P)
        diag2 = view(12288, KC, P)
        diag_moe = view(15360, KC, P)

        moe_ring = ring + [view(4096 * j, KC, 512) for j in range(3)]
        ex_hT = view(12288, KC, P)
        ex_sg = view(13312, 2, GU)
        ex_hb = view(13824, 2, GU)
        ex_ff = view(14336, 4, 2, P)
        ex_y = view(15360, D)
        y_acc = mixT[:, 0:4, :].rearrange("p a b -> p (a b)").rearrange("p (t n) -> p t n", t=2)
        pick = mixT[:, 4, 0:256].rearrange("p (t s) -> p t s", t=2)
        pick_w = mixT[:, 4, 256:512].rearrange("p (t s) -> p t s", t=2)
        pick_wT = mixT[:, 5, 0:256]
        iota = mixT[:, 5, 256:512]
        router = mixT[:, 6, 0:64].rearrange("p (k e) -> p k e", e=E_)
        router_bias = mixT[:, 6, 64:72]
        rt = mixT[:, 7, :].rearrange("p (n t e) -> p n t e", t=2, e=E_)
        flag = sb("overflow", [P, 1], I32)

        k_tok = view(0, 4, 2, HG)
        lf_tok = view(4096, 4, 2, HG)
        qT = view(8192, HEADS, 4 * P)
        v_tok = view(10240, 4, HG)
        dvft = view(12288, 4, 512)
        g_tok = view(14336, 4, HG)
        hT_flat = hT[:, :, :].rearrange("p k t -> p (k t)")
        mix_flat = mixT[:, :, :].rearrange("p k t -> p (k t)")
        xn_flat = xn[:, :, :].rearrange("p s n -> p (s n)")
        gate_flat = gate_bc[:, :, :].rearrange("p s n -> p (s n)")

        def part(flat, off, *shape):
            n = int(np.prod(shape))
            names = "abcd"[:len(shape)]
            v = flat[:, off:off + n]
            if len(shape) > 1:
                v = v.rearrange(f"p ({' '.join(names)}) -> p {' '.join(names)}",
                                **{c: s for c, s in zip(names[1:], shape[1:])})
            return v

        o_tok = part(hT_flat, 0, 4, HG)
        decay = part(hT_flat, 2048, 2, HG)
        qw = part(hT_flat, 3072, 2, HG)
        kw = part(mix_flat, 0, 2, HG)
        state = part(mix_flat, 1024, 2, HEADS, P)
        dqk = part(mix_flat, 0, 4, 512)
        bounds = part(mix_flat, 2048, 2, 2, HG)
        bound_tmp = view(14336, 2, HG)
        dqkT = part(xn_flat, 0, 4, 512)
        b_T = part(xn_flat, 0, HG)
        k_T = part(xn_flat, 512, HG)
        q_in = part(xn_flat, 1024, HG)
        k_out = part(xn_flat, 1536, HG)
        dft_tok = part(gate_flat, 0, TX, 512)
        dft_ch = part(gate_flat, 1024, 2, P)
        fu = part(gate_flat, 1280, 512)
        b_exp = [part(gate_flat, 0, HG), part(gate_flat, 1536, HG)]
        scores = part(gate_flat, 512, 2, HG)
        probs = part(hT_flat, 2048, 2, 512)
        weights = part(hT_flat, 3072, 2, 512)
        od_tok = part(hT_flat, 0, 4, 256)
        wT = part(hT_flat, 1024, 2, 4, P)
        rope_tmp = part(hT_flat, 2048, 2, 512)
        row_par = sb("row_par", [P, 320])
        onorm, subln = row_par[:, 0:P], row_par[:, P:P + 64]
        lam4 = row_par[:, 192:320]

        psum = ctx.enter_context(nc.psum_tensor("banks", [P, 8, 512], F32))

        landed = [sem(f"landed{j}") for j in range(7)]
        freed = [sem(f"freed{j}") for j in range(7)]
        consts_in = sem("consts_in")
        packs_turned = sem("packs_turned")
        cols_ready = sem("cols_ready")
        cond_ready = sem("cond_ready")
        rows_ready = sem("rows_ready")
        rows_copied = sem("rows_copied")
        mods_turned = sem("mods_turned")
        mods_ready = sem("mods_ready")
        narrow_in = [sem(f"narrow_in{h}") for h in range(2)]
        narrow_used = sem("narrow_first_half_used")
        narrow_summed = sem("narrow_summed")
        narrow_spread = sem("narrow_columns")
        narrow_copied = sem("narrow_copied")
        narrow_link = sem("narrow_link")
        diag_ready = sem("diag_ready")
        gate_spread = sem("gate_spread")
        gate_ready = sem("gate_ready")
        x_ready = sem("x_ready")
        ss_ready = sem("ss_ready")
        xn_ready = sem("xn_ready")
        xn_turned = sem("xn_turned")
        hT_act = sem("hT_act")
        hT_dve = sem("hT_dve")
        proj = sem("proj_ready")
        dve_link = sem("dve_link")
        act_link = sem("act_link")
        glu_sig = sem("glu_sig")
        glu_done = sem("glu_done")
        pool_in = sem("pool_in")
        sgu_turned = sem("sgu_turned")
        act_copied = sem("act_copied")
        v_normed = sem("v_normed")
        pool_diff = sem("pool_diff")
        diff_copied = sem("diff_copied")
        pool_out = sem("pool_out")
        sgu_mixed = sem("sgu_mixed")
        sgu_gated = sem("sgu_gated")
        conv_done = sem("conv_done")
        conv_sum = sem("conv_sum")
        conv_centred = sem("conv_centred")
        conv_squared = sem("conv_squared")
        conv_ssum = sem("conv_ssum")
        conv_normed = sem("conv_normed")
        mix_ready = sem("mix_ready")
        w_out_done = sem("w_out_done")
        gu_done = sem("gu_done")
        silu_done = sem("silu_done")
        hb_done = sem("hb_done")
        hb_turned = sem("hb_turned")
        ff_ready = sem("ff_ready")
        down_done = sem("down_done")
        y_copied = sem("y_copied")
        logits = sem("logits")
        route_exp_in = sem("route_exp_in")
        route_exp = sem("route_exp")
        selected = sem("selected")
        positions = sem("positions")
        routed = sem("routed")
        picked = sem("picked")
        gathered = sem("gathered")
        pick_turned = sem("pick_turned")
        pick_wT_ready = sem("pick_wT_ready")
        ex_act = sem("ex_act")
        ex_dve = sem("ex_dve")
        ex_y_done = sem("ex_y_done")
        ex_y_copied = sem("ex_y_copied")
        scattered = sem("scattered")
        stored = sem("stored")
        var_ready = sem("var_ready")
        root_ready = sem("root_ready")
        late_in = sem("late_in")
        pool_cleared = sem("pool_cleared")
        ones_set = sem("ones_set")
        router_in = sem("router_in")
        gu_done_e = sem("expert_gu_done")
        silu_done_e = sem("expert_silu_done")
        hb_done_e = sem("expert_hb_done")
        hb_turned_e = sem("expert_hb_turned")
        ff_ready_e = sem("expert_ff_ready")
        moe_link = sem("moe_link")
        landed2 = [sem(f"second_landed{j}") for j in range(SLOTS)]
        freed2 = [sem(f"second_freed{j}") for j in range(SLOTS)]

        def landed_of(L):
            return landed if L < 2 else landed2

        def freed_of(L):
            return freed if L < 2 else freed2

        def cond_of(L, s):
            return 0 if L < 2 else 1 + s

        def narrow_buf(M, h):
            if M == 2:
                return hT[:, 2 * h:2 * h + 2, :].rearrange("p a b -> p (a b)").rearrange("p (k n) -> p k n", k=4)
            return xn[:, h, :].rearrange("p (k n) -> p k n", k=4)

        def streams_of(M):
            return (0, 1) if M < 2 else (1, 2)

        def narrow_per_pass(L):
            M = L + 1
            if M > max(stages):
                return 0
            return (NARROW_ALL - narrow_first(M) - NARROW_TAIL[L]) // (E_ if L == 1 else 2)

        def narrow_tail(L):
            return (NARROW_TAIL[L] if L + 1 <= max(stages) else 0), 2 * narrow_per_pass(L)

        def gain_cols(L, i):
            lo = 16 * i + KC * L if L < 2 else 32 + KC * (4 * (L - 2) + 2 * i)
            return cols[:, lo:lo + KC]

        def post_cols(L, i):
            lo = 32 + KC * (4 * (L - 2) + 2 * i + 1)
            return cols[:, lo:lo + KC]

        PACKS = [(96, 0), (22, 96), (96, 118), (96, 214)]
        SGU_BANK = (4, 5, 2)
        LOGIT, TOP, EQ1, CUM, SEL1, EQ2, SEL2, SEL, DIFF, EXPD, W1, W2, COMB, POS = range(14)
        loaded = {}
        final_gain = gate_bc[:, 1, :]

        params2_in = sem("params2_in")
        bounds_exp_in = sem("bounds_exp_in")
        bounds_exp = sem("bounds_exp")
        lam_in = sem("lam_in")
        lam_exp = sem("lam_exp")
        in_copied = sem("in_copied")
        forget_ready = sem("forget_ready")
        log_ready = sem("log_ready")
        roped = sem("roped")
        dqk_turned = sem("dqk_turned")
        dqkT_ready = sem("dqkT_ready")
        fourier_ps = sem("fourier_ps")
        fourier_sb = sem("fourier_sb")
        attn_scores = sem("attn_scores")
        attn_max = sem("attn_max")
        attn_exp = sem("attn_exp")
        attn_w = sem("attn_w")
        attn_wT = sem("attn_wT")
        attn_wT_sb = sem("attn_wT_sb")
        attn_o = sem("attn_o")
        attn_o_sb = sem("attn_o_sb")
        head_ss = sem("head_ss")
        out_normed = sem("out_normed")
        out_turned = sem("out_turned")
        out_copied = sem("out_copied")
        scan_in = sem("scan_in")
        scan_sb = sem("scan_sb")
        scan_kd = sem("scan_kd")
        level_arg = sem("level_arg")
        level_exp = sem("level_exp")
        level_qk = sem("level_qk")
        level_ps = sem("level_ps")
        level_put = sem("level_put")
        scan_o = sem("scan_o")
        scan_done = sem("scan_done")
        SCAN = [(0, 2), (1, 3), (0, 3), (1, 2), (0, 0), (1, 1), (0, 1), (1, 0)]
        FIRST = {2: 0, 3: 1, 0: 0, 1: 1}
        MX, NMX, DEN, RDEN, LAM, HS = 24, 26, 28, 30, 32, 36

        def post_bank(sem, n, t, T):
            if sem is w_out_done:
                return 4 * n + t if T == 4 else (2, 3, 6, 7)[2 * n + t]
            return t if T == 4 else 2 * n + t

        def start_x(L):
            return 2 + sum(2 * T_OUT[m] for m in stages if m < L) + 4

        LAST1 = min(1, max(stages))

        def TOTAL_X():
            return 2 + sum(2 * T_OUT[L] for L in stages) + 4
        XR = {1: 8 if 0 in stages else 4}

        block = ctx.enter_context(nc.Block())

        ada = [a["ada_w"][l].rearrange("(p k) n -> p k n", k=KC) for l in range(2)] + \
              [a["w_mod_2"][l].rearrange("(p k) n -> p k n", k=KC) for l in range(2)]
        w_in1 = [a["w_in"][l].rearrange("(k p) n -> p k n", p=P) for l in range(2)]
        w_out1 = [a["w_out"][l].rearrange("(k p) n -> p k n", p=P) for l in range(2)]
        w_in2 = [a["w_in_2"][l].rearrange("(k p) n -> p k n", p=P) for l in range(2)]
        w_out2 = [a["w_out_2"][l].rearrange("(k p) n -> p k n", p=P) for l in range(2)]
        ffn_gate = a["ffn_w_gate"][0].rearrange("(k p) n -> p k n", p=P)
        ffn_up = a["ffn_w_up"][0].rearrange("(k p) n -> p k n", p=P)
        ffn_down = a["ffn_w_down"][0].rearrange("(k p) n -> p k n", p=P)
        ffn2_in = [a["w_ffn_in_2"][l].rearrange("(k p) n -> p k n", p=P) for l in range(2)]
        ffn2_down = [a["w_ffn_out_2"][l].rearrange("(k p) n -> p k n", p=P) for l in range(2)]
        moe_gate = a["moe_w_gate"][0].rearrange("e (k p) n -> e p k n", p=P)
        moe_up = a["moe_w_up"][0].rearrange("e (k p) n -> e p k n", p=P)
        moe_down = a["moe_w_down"][0].rearrange("e (k p) n -> e p k n", p=P)

        C1_COLS = [(256, 384), (640, 384), (0, 256), (1408, 384), (1024, 384)]
        C2_COLS = [1536, 2048, 512, 0, 2560, 3072, 1024]
        DOWN = [(n, kb) for n in range(2) for kb in range(3)]
        T_IN = [2, 2, 4, 4]
        T_OUT = [2, 2, 4, 2]
        slot_k1024 = [w.rearrange("p k n -> p (k n)").rearrange("p (k n) -> p k n", n=D)
                      for w in [r[:, :, :] for r in ring] + moe_ring[SLOTS:]]
        slot_k512 = [r[:, :, :] for r in ring] + moe_ring[SLOTS:]

        @block.sync
        def _(sp):
            c = Count()
            L = 0

            def const(dst, src, sem=late_in):
                sp.dma_start(dst, src).then_inc(sem, 16)
                loaded[id(sem)] = loaded.get(id(sem), 0) + 16

            def claim(j, it=0, step=0):
                frd = freed_of(L)[j]
                sp.wait_ge(frd, it + (c.at(frd) + step + 1))

            def plain(j, src):
                k = src.shape[1]
                h = (k + 1) // 2
                claim(j)
                for lo, hi in ((0, h), (h, k)):
                    sp.dma_start(ring[j][:, lo:hi, 0:src.shape[2]], src[:, lo:hi, :]).then_inc(landed_of(L)[j], 16)
                c.up(freed_of(L)[j])

            def mods(M):
                if not MOD_BLOCKS[M]:
                    return
                with sp.Fori(0, MOD_BLOCKS[M] // SLOTS) as it:
                    for j in range(SLOTS):
                        claim(j, it)
                        for h in range(2):
                            sp.dma_start(ring[j][:, 4 * h:4 * h + 4, :],
                                         ada[M][:, 4 * h:4 * h + 4, bass.ds(it * (SLOTS * 512) + j * 512, 512)])\
                                .then_inc(landed_of(L)[j], 16)
                for j in range(SLOTS):
                    c.up(freed_of(L)[j], MOD_BLOCKS[M] // SLOTS)

            def ffn(gate, up, down):
                def both(j, o, it=0):
                    claim(j, it)
                    sp.dma_start(ring[j][:, :, 0:GU], gate[:, :, bass.ds(o, GU)]).then_inc(landed_of(L)[j], 16)
                    sp.dma_start(ring[j][:, :, GU:512], up[:, :, bass.ds(o, GU)]).then_inc(landed_of(L)[j], 16)
                with sp.Fori(0, 2) as it:
                    for j in range(SLOTS):
                        both(j, it * (SLOTS * GU) + j * GU, it)
                for j in range(SLOTS):
                    c.up(freed_of(L)[j], 2)
                for b in range(8, 11):
                    both(b % SLOTS, b * GU)
                    c.up(freed_of(L)[b % SLOTS])
                for s, (n, kb) in enumerate(DOWN):
                    plain((s + 3) % SLOTS, down[:, kb * 8:min(kb * 8 + 8, FFC), n * 512:(n + 1) * 512])

            def moe(batch):
                with sp.Fori(0, E_) as e:
                    for s, (kind, g) in enumerate(MOE_ORDER):
                        j, rank = s % 7, s // 7
                        claim(j, e * 3, rank)
                        if s == SLOTS:
                            sp.wait_ge(x_ready, XR[1])
                        if kind == "gu":
                            for h, w in ((0, moe_gate), (1, moe_up)):
                                sp.dma_start(slot_k512[j][:, :, h * GU:(h + 1) * GU],
                                             w[bass.ds(e, 1), :, :, g * GU:(g + 1) * GU]).then_inc(landed_of(L)[j], 16)
                        else:
                            for h in range(2):
                                sp.dma_start(slot_k1024[j][:, 2 * h:2 * h + 2, :],
                                             moe_down[bass.ds(e, 1), :, 4 * g + 2 * h:4 * g + 2 * h + 2, :])\
                                    .then_inc(landed_of(L)[j], 16)
                for j in range(7):
                    c.up(freed_of(L)[j], 3 * E_)

            for n, name in enumerate(("c", "c_2", "c_ctx_2")):
                src = a[name] if len(a[name].shape) == 1 else a[name][0]
                const(cond_raw[:, n, :], src.rearrange("(p k) -> p k", k=KC), consts_in)
            const(ident[:, :], a["k_ident"], consts_in)
            for row, n, src in ((0, 0, a["mix_norm_g"]), (16, 0, a["ffn_norm_g"]), (0, 1, a["pool_scale"]),
                                (4, 1, a["conv_b"]), (10, 1, a["conv_ln_g"]), (16, 1, a["conv_ln_b"]),
                                (0, 2, a["ada_b"]), (0, 3, a["b_mod_2"])):
                src = src.rearrange("l (k p) -> (l k) p", p=P)
                const(packs[row:row + src.shape[0], n, :], src, consts_in)
            const(packs[32:96, 0, :], a["norm_g_2"].rearrange("l n (k p) -> (l n k) p", p=P), consts_in)
            for l in range(2):
                const(conv_raw[0:TAPS, l * CONV_W:(l + 1) * CONV_W], a["conv_w"][l], consts_in)
            mods(0)
            const(x[:, 0:2, :], a["x"][0].rearrange("(t p) n -> p t n", p=P))
            const(band, a["k_band"].rearrange("(t p) g n -> p t (g n)", p=P))
            const(sgu_raw, a["sgu_w"].rearrange("l h p q -> p (l h) q"))
            const(sgu_bias[0:1, :], a["sgu_b"].rearrange("(o l) h p -> o (l h p)", o=1))
            for l in range(2):
                for n, name in enumerate(("sgu_ln_g", "sgu_ln_b")):
                    const(sgu_ln[:, 2 * l + n, :], a[name][l:l + 1, :].to_broadcast((P, SGU_W)))
            sp.wait_ge(pool_cleared, 1)
            for l in range(2):
                for g in range(4):
                    h = g % 2
                    const(pool_bd[64 * h:64 * h + 64, 2 * l + g // 2, 64 * h:64 * h + 64], a["pool_w"][l, g])
            const(final_gain, a["final_norm_g"].rearrange("(o n) -> o n", o=1).to_broadcast((P, D)))
            const(tri[:, :, :], a["k_tri"])
            const(mask_words[:, :], a["k_masks"])
            const(x[:, 2:4, :], a["ctx_2"][0].rearrange("(t p) n -> p t n", p=P))
            const(rope[:, :, :, :], a["k_rope"].rearrange("(t p) s n -> p t s n", p=P))
            for L in stages:
                if L < 2:
                    for s, (lo, w) in enumerate(C1_COLS):
                        plain(s % SLOTS, w_in1[L][:, :, lo:lo + w])
                    if L + 1 <= max(stages):
                        mods(L + 1)
                    for n in range(2):
                        plain(n, w_out1[L][:, :, n * 512:(n + 1) * 512])
                else:
                    l = L - 2
                    for s, lo in enumerate(C2_COLS[:SLOTS]):
                        plain(s, w_in2[l][:, :, lo:lo + 512])
                    sp.wait_ge(x_ready, start_x(L))
                    for dst, src in ((dft_tok, a["k_dft_tok"].rearrange("(t p) n -> p t n", p=P)),
                                     (dft_ch, a["k_dft_ch"]),
                                     (onorm, a["hg_onorm_2"][l:l + 1, :].to_broadcast((P, P))),
                                     (subln, a["da_subln_2"][l:l + 1, :].to_broadcast((P, 64))),
                                     (lam4, a["da_lambda_2"][l:l + 1].rearrange("o n d -> o (n d)").to_broadcast((P, P)))):
                        sp.dma_start(dst, src).then_inc(params2_in, 16)
                    if l:
                        src = a["hg_lb_logits_2"].rearrange("(o d) l n -> o (d l n)", o=1).to_broadcast((P, 4 * HG))
                        sp.dma_start(bounds.rearrange("p d l n -> p (d l n)"), src).then_inc(params2_in, 16)
                    for s, lo in enumerate(C2_COLS[SLOTS:]):
                        plain(s % SLOTS, w_in2[l][:, :, lo:lo + 512])
                    if L + 1 <= max(stages):
                        mods(L + 1)
                    for n in range(2):
                        plain(n, w_out2[L - 2][:, :, n * 512:(n + 1) * 512])
                if L == 0:
                    ffn(ffn_gate, ffn_up, ffn_down)
                if L == 1:
                    moe(0)
                    sp.wait_ge(routed, 1)
                    over = sp.value_load(flag[0:1, 0:1], min_val=0, max_val=1)
                    with sp.If(over > 0):
                        moe(1)
                        for j in range(7):
                            sp.wait_ge(freed[j], c.at(freed[j]) + 1)
                    for j in range(7):
                        sp.wait_ge(freed[j], c.at(freed[j]) - 3 * E_ + 1)
                if L >= 2:
                    ffn(ffn2_in[L - 2][:, :, 0:FF], ffn2_in[L - 2][:, :, FF:2 * FF], ffn2_down[L - 2])
            for t in range(TX):
                sp.wait_ge(x_ready, TOTAL_X() - TX + 1 + t)
                sp.dma_start(out[0, t * P:(t + 1) * P, :], x[:, t, :]).then_inc(stored, 16)
            sp.wait_ge(stored, 16 * TX)
        def banks(lo, n=1):
            return psum[:, lo, :] if n == 1 else psum[:, lo:lo + n, :]

        PAR2 = {2: 80, 3: 80 + 96} if 2 in stages else {3: 96}
        CONSTS, LATE = loaded[id(consts_in)], loaded[id(late_in)]

        @block.tensor
        def _(pe):
            c = Count()
            owed = []

            def tag(ins):
                if owed:
                    ins.then_inc(owed.pop(0), 1)
                return ins

            def pay(bank):
                while owed:
                    tag(pe.matmul(psum[0:1, bank, 510:512], ones[:, 0:1], ones[:, 0:2], start=True, stop=True))

            def transpose(dst, src, n=P):
                return pe.transpose(dst, src, ident[0:n, 0:n])

            def take(j, L):
                pe.wait_ge(landed_of(L)[j], c.up(landed_of(L)[j], 32))

            def mods(L):
                if not MOD_BLOCKS[L]:
                    return
                frd = freed_of(L - 1)
                lnd = landed_of(L - 1)
                mod_ps = psum[:, 3, :]

                def turn(n_abs, buf):
                    pe.wait_ge(rows_copied, c.up(rows_copied))
                    for q in range(4):
                        dst = mod_ps[:, bass.ds(n_abs * 12 + q * 3, 3)]
                        ins = pe.matmul(dst, rows[:, buf, q * P:(q + 1) * P], ident[0:3, 0:3], start=True, stop=True)
                        if q == 0:
                            tag(ins)
                    return ins

                assert not owed
                with pe.Fori(0, MOD_BLOCKS[L] // SLOTS) as it:
                    c.begin(it, (rows_copied, SLOTS), *[(lnd[j], 32) for j in range(SLOTS)])
                    for j in range(SLOTS):
                        pe.wait_ge(lnd[j], c.up(lnd[j], 32))
                        for k in range(KC):
                            mm = pe.matmul(psum[0:3, j % 2, :], cond[:, k, :], ring[j][:, k, :],
                                           start=(k == 0), stop=(k == KC - 1))
                            if k == 0:
                                tag(mm)
                        mm.then_inc(rows_ready, 1)
                        if j:
                            turn(it * SLOTS + (j - 1), (j - 1) % 2)
                        owed.append(frd[j])
                    ins = turn(it * SLOTS + (SLOTS - 1), (SLOTS - 1) % 2)
                    ins.then_inc(mods_turned, 1)
                    c.end(MOD_BLOCKS[L] // SLOTS)

            def narrow_columns(M, blocks, bank):
                ns = streams_of(M)[1]
                for i, b in enumerate(blocks):
                    pe.wait_ge(narrow_summed, c.up(narrow_summed))
                    for q in range(2):
                        for s in range(ns):
                            n = GU + (2 * i + q) * ns + s
                            mm = pe.matmul(psum[:, bank, n:n + 1], mod_sum[:, b % 2, s, q * P:(q + 1) * P], ones[:, 0:1],
                                           start=True, stop=True)
                    mm.then_inc(narrow_spread, 1)

            def spread(first_bank, diag):
                pe.wait_ge(diag_ready, c.up(diag_ready))
                for h in range(2):
                    mm = pe.matmul(psum[:, first_bank + h, :], ones[:, :],
                                   diag[:, 4 * h:4 * h + 4, :].rearrange("p k f -> p (k f)"),
                                   start=True, stop=True)
                    if h == 0:
                        tag(mm)
                mm.then_inc(gate_spread, 1)

            def norm_turn(T):
                for t in range(T):
                    pe.wait_ge(xn_ready, c.up(xn_ready))
                    if t:
                        pe.wait_ge(hT_act, c.up(hT_act))
                        pe.wait_ge(hT_dve, c.up(hT_dve))
                    for k in range(KC):
                        tr = transpose(psum[:, 4 + k // 4, (k % 4) * P:(k % 4 + 1) * P],
                                       xn[:, t % 2, k * P:(k + 1) * P])
                        if k < KC - 1:
                            tag(tr)
                    tr.then_inc(xn_turned, 1)
                pe.wait_ge(hT_act, c.up(hT_act))
                pe.wait_ge(hT_dve, c.up(hT_dve))

            def project_T(j, L, chunks, T, place, sem):
                take(j, L)
                for ch in range(chunks):
                    for k in range(KC):
                        mm = pe.matmul(place(ch), ring[j][:, k, ch * P:(ch + 1) * P], hT[:, k, 0:T * P],
                                       start=(k == 0), stop=(k == KC - 1))
                        if k < KC - 1:
                            tag(mm)
                mm.then_inc(sem, 1)
                owed.append(freed_of(L)[j])

            def project(j, L, w, tiles, place, sem, src=hT):
                take(j, L)
                for t in tiles:
                    for k in range(KC):
                        mm = pe.matmul(place(t), src[:, k, t * P:(t + 1) * P], ring[j][:, k, 0:w],
                                       start=(k == 0), stop=(k == KC - 1))
                        if k < KC - 1:
                            tag(mm)
                    mm.then_inc(sem, 1)
                owed.append(freed_of(L)[j])

            def mixer1(L):
                project_T(0, L, CC, TX, lambda ch: psum[:, ch // 2, (ch % 2) * SEQ:(ch % 2 + 1) * SEQ], proj)
                project_T(1, L, CC, TX, lambda ch: psum[:, 2 + ch // 2, (ch % 2) * SEQ:(ch % 2 + 1) * SEQ], proj)
                project(2, L, POOL_W, range(TX), lambda t: psum[:, 6 + t, 0:POOL_W], pool_in)
                project(3, L, SGU_W, range(TX), lambda t: psum[:, 4 + t, 0:SGU_W], proj)
                pe.wait_ge(glu_done, c.up(glu_done))
                project_T(0, L, CC, TX, lambda ch: psum[:, ch // 2, (ch % 2) * SEQ:(ch % 2 + 1) * SEQ], proj)
                for h in range(SGU_HEADS):
                    tr = transpose(psum[:, 2 + h // 4, (h % 4) * P:(h % 4 + 1) * P], sgu_raw[:, L * SGU_HEADS + h, :])
                    if h == 0:
                        tag(tr)
                tr.then_inc(sgu_turned, 1)
                pe.wait_ge(act_copied, c.up(act_copied))
                for j in range(2):
                    for t in range(TX):
                        mm = pe.matmul(psum[:, 6 + j, :], pool_tok[:, t, j * P:(j + 1) * P],
                                       band[:, t, j * 512:(j + 1) * 512], start=(t == 0), stop=(t == TX - 1))
                mm.then_inc(pool_diff, 1)
                pe.wait_ge(diff_copied, c.up(diff_copied))
                for j in range(2):
                    mm = pe.matmul(psum[:, 6 + j, 0:SEQ], pool_bd[:, 2 * L + j, :], diffT[:, j, :], start=True, stop=True)
                mm.then_inc(pool_out, 1)
                pe.wait_ge(act_copied, c.up(act_copied, 2))
                pe.wait_ge(v_normed, c.up(v_normed))
                for n in range(TX * CC):
                    t, j = n // CC, n % CC
                    dst = psum[:, SGU_BANK[n // 2], (n % 2) * SEQ:(n % 2 + 1) * SEQ]
                    pe.matmul(dst, v_n[:, t, j * P:(j + 1) * P],
                              sgu_wT[:, 2 * j:2 * j + 2, :].rearrange("p h q -> p (h q)"), start=True, stop=False)
                    lo = (L * SGU_HEADS + 2 * j) * P
                    mm = pe.matmul(dst, ones[0:1, :], sgu_bias[0:1, lo:lo + 2 * P], start=False, stop=True)
                mm.then_inc(sgu_mixed, 1)
                if L + 1 <= max(stages):
                    mods(L + 1)
                pe.wait_ge(conv_done, c.up(conv_done))
                for ch in range(CC):
                    mm = pe.matmul(psum[:, 0, 0:SEQ], ones[:, :], conv_y[:, ch, :], start=(ch == 0), stop=(ch == CC - 1))
                mm.then_inc(conv_sum, 1)
                pe.wait_ge(conv_squared, c.up(conv_squared))
                for ch in range(CC):
                    mm = pe.matmul(psum[:, 1, 0:SEQ], ones[:, :], conv_sq[:, ch, :], start=(ch == 0), stop=(ch == CC - 1))
                mm.then_inc(conv_ssum, 1)

            def out_proj(L, T):
                for n in range(2):
                    project(n, L, 512, range(T), lambda t: psum[:, 4 * n + t if T == 4 else (2, 3, 6, 7)[2 * n + t], :],
                            w_out_done, mixT)

            def mixer2(L):
                W = T_OUT[L]
                for n in range(7):
                    base = 4 * (n % 2)

                    def place(t):
                        if n >= 2:
                            pe.wait_ge(in_copied, c.up(in_copied))
                        return psum[:, base + t, :]
                    if n == 3:
                        j = n % SLOTS
                        take(j, L)
                        for h in range(HEADS):
                            dst = place(h)[:, 0:W * P]
                            for k in range(KC):
                                mm = pe.matmul(dst, ring[j][:, k, h * P:(h + 1) * P], hT[:, k, 0:W * P],
                                               start=(k == 0), stop=(k == KC - 1))
                                if k < KC - 1:
                                    tag(mm)
                            mm.then_inc(proj, 1)
                        owed.append(freed_of(L)[j])
                    else:
                        project2(n % SLOTS, L, range(W if n == 6 else 4), place)
                pe.wait_ge(in_copied, c.up(in_copied, 8))
                pay(0)
                if L + 1 <= max(stages):
                    mods(L + 1)
                pe.wait_ge(roped, c.up(roped))
                for ch in range(4):
                    for t in range(4):
                        tr = transpose(psum[:, 4 + ch, t * P:(t + 1) * P], dqk[:, t, ch * P:(ch + 1) * P])
                tr.then_inc(dqk_turned, 1)
                pe.wait_ge(params2_in, PAR2[L])
                for s in range(W // 2):
                    for j in range(2):
                        for t in range(TX):
                            lo = 256 + j * P
                            mm = pe.matmul(psum[:, 0, :], dvft[:, 2 * s + t, lo:lo + P], dft_tok[:, t, :],
                                           start=(t == 0), stop=(t == TX - 1))
                        mm.then_inc(fourier_ps, 1)
                        pe.wait_ge(fourier_sb, c.up(fourier_sb))
                        for r in range(2):
                            mm = pe.matmul(psum[:, 1, 0:SEQ], dft_ch[:, r, :], fu[:, r * SEQ:(r + 1) * SEQ],
                                           start=(r == 0), stop=(r == 1))
                        mm.then_inc(fourier_ps, 1)
                        pe.wait_ge(fourier_sb, c.up(fourier_sb))
                pe.wait_ge(dqkT_ready, c.up(dqkT_ready))
                units = [(t, h) for t in range(W) for h in range(HEADS)]

                def attend(u):
                    t, h = units[u]
                    k0 = 0 if t < TX else SEQ
                    for m in range(2):
                        r, ch = 32 * ((2 * h + m) % 4), (2 * h + m) // 4
                        mm = pe.matmul(psum[:, 2 * (u % 2) + m, 0:512 - k0], dqkT[r:r + 32, ch, t * P:(t + 1) * P],
                                       dqkT[r:r + 32, 2 + ch, k0:512], start=True, stop=True)
                    mm.then_inc(attn_scores, 1)

                def turn_weights(u):
                    t, h = units[u]
                    pe.wait_ge(attn_w, c.up(attn_w))
                    for kt in range(4 if t < TX else 2):
                        tr = transpose(psum[:, 4 + u % 2, kt * P:(kt + 1) * P], weights[:, u % 2, kt * P:(kt + 1) * P])
                    tr.then_inc(attn_wT, 1)

                def values(u):
                    t, h = units[u]
                    pe.wait_ge(attn_wT_sb, c.up(attn_wT_sb))
                    if h == 0 and t >= 2:
                        pe.wait_ge(attn_o_sb, c.up(attn_o_sb))
                    kts = range(4) if t < TX else range(2, 4)
                    for n, kt in enumerate(kts):
                        mm = pe.matmul(psum[:, 6 + t % 2, h * 64:(h + 1) * 64], wT[:, u % 2, n, :],
                                       dvft[:, kt, h * 64:(h + 1) * 64], start=(n == 0), stop=(n == len(kts) - 1))
                    mm.then_inc(attn_o, 1)

                for u in range(len(units) + 2):
                    if u < len(units):
                        attend(u)
                    if 0 <= u - 1 < len(units):
                        turn_weights(u - 1)
                    if 0 <= u - 2 < len(units):
                        values(u - 2)
                pe.wait_ge(attn_o_sb, c.up(attn_o_sb, 2))
                for t in range(W):
                    pe.wait_ge(out_normed, c.up(out_normed))
                    if t >= 2:
                        pe.wait_ge(out_copied, c.up(out_copied))
                    for j in range(2):
                        tr = transpose(psum[:, 4 + t % 2, j * P:(j + 1) * P], od_tok[:, t, j * P:(j + 1) * P])
                    tr.then_inc(out_turned, 1)
                pe.wait_ge(out_copied, c.up(out_copied, 2))
                pe.wait_ge(log_ready, c.up(log_ready))
                seen = set()

                def scan_inputs(i):
                    d, t = SCAN[i]
                    for h in range(HEADS):
                        pe.matmul(psum[:, 0, h * P:(h + 1) * P], lf_tok[:, t, d, h * P:(h + 1) * P], tri[:, d, :],
                                  start=True, stop=True)
                    mm = pe.matmul(psum[:, 1, :], tri[:, 2 + d, :], lf_tok[:, t, d, :], start=True, stop=True)
                    if t < W:
                        for h in range(HEADS):
                            mm = transpose(psum[:, 2, h * P:(h + 1) * P], k_tok[:, t, d, h * P:(h + 1) * P])
                    mm.then_inc(scan_in, 1)

                def state_part(d, t):
                    pe.wait_ge(scan_kd, c.up(scan_kd))
                    for h in range(HEADS):
                        mm = pe.matmul(psum[:, 3, h * P:(h + 1) * P], k_tok[:, t, d, h * P:(h + 1) * P],
                                       v_tok[:, t, h * P:(h + 1) * P], start=True, stop=True)
                    mm.then_inc(scan_o, 1)

                scan_inputs(0)
                for i, (d, t) in enumerate(SCAN):
                    want = t < W
                    pe.wait_ge(scan_sb, c.up(scan_sb))
                    if want:
                        for h in range(HEADS):
                            mm = pe.matmul(psum[:, 6, h * P:(h + 1) * P], k_T[:, h * P:(h + 1) * P],
                                           qT[:, h, t * P:(t + 1) * P], start=True, stop=True)
                        mm.then_inc(level_ps, 1)
                        state_part(d, t)
                        for lv in range(LEVELS):
                            if lv == 2 and i + 1 < len(SCAN):
                                scan_inputs(i + 1)
                            pe.wait_ge(level_qk, c.up(level_qk))
                            if lv >= 2:
                                pe.wait_ge(level_put, c.up(level_put, 2 if lv == 2 else 1))
                            for h in range(HEADS):
                                mm = pe.matmul(psum[:, 4 + lv % 2, h * P:(h + 1) * P], kw[:, lv % 2, h * P:(h + 1) * P],
                                               qw[:, lv % 2, h * P:(h + 1) * P], start=True, stop=True)
                            mm.then_inc(level_ps, 1)
                        pe.wait_ge(level_put, c.up(level_put, 2))
                        for h in range(HEADS):
                            if d in seen:
                                pe.matmul(psum[:, 7, h * P:(h + 1) * P], q_in[:, h * P:(h + 1) * P], state[:, d, h, :],
                                          start=True, stop=False)
                            mm = pe.matmul(psum[:, 7, h * P:(h + 1) * P], scores[:, d, h * P:(h + 1) * P],
                                           v_tok[:, t, h * P:(h + 1) * P], start=d not in seen, stop=True)
                        mm.then_inc(scan_o, 1)
                    else:
                        if i + 1 < len(SCAN):
                            scan_inputs(i + 1)
                        state_part(d, t)
                    seen.add(d)
                    pe.wait_ge(scan_done, c.up(scan_done))
                for t in range(W):
                    pe.wait_ge(out_normed, c.up(out_normed))
                    if t >= 2:
                        pe.wait_ge(out_copied, c.up(out_copied))
                    for h in range(HEADS):
                        tr = transpose(psum[:, 4 + t % 2, h * P:(h + 1) * P], o_tok[:, t, h * P:(h + 1) * P])
                    tr.then_inc(out_turned, 1)
                pe.wait_ge(out_copied, c.up(out_copied, 2))

            def project2(j, L, tiles, place):
                take(j, L)
                for t in tiles:
                    dst = place(t)
                    for k in range(KC):
                        mm = pe.matmul(dst, hT[:, k, t * P:(t + 1) * P], ring[j][:, k, :],
                                       start=(k == 0), stop=(k == KC - 1))
                        if k < KC - 1:
                            tag(mm)
                    mm.then_inc(proj, 1)
                owed.append(freed_of(L)[j])

            def ffn(L, T):
                ffT, _, _ = ff_space(T)
                lnd, frd = landed_of(L), freed_of(L)

                def turn(u, ends=()):
                    pe.wait_ge(hb_done, c.up(hb_done))
                    if u and ends:
                        narrow_columns(L + 1, ends[u - 1], 4 + u % 2)
                    for q in range(2):
                        tr = transpose(psum[:, 4 + u % 2, q * P:(q + 1) * P], hb[:, u % 2, q * P:(q + 1) * P])
                        if q == 0:
                            tag(tr)
                    tr.then_inc(hb_turned, 1)

                def units(blocks, ends=()):
                    u = 0
                    for j in range(blocks):
                        pe.wait_ge(lnd[j], c.up(lnd[j], 32))
                        for t in range(T):
                            for k in range(KC):
                                mm = pe.matmul(psum[:, u % 4, :], hT[:, k, t * P:(t + 1) * P], ring[j][:, k, :],
                                               start=(k == 0), stop=(k == KC - 1))
                            mm.then_inc(gu_done, 1)
                            if t == T - 1:
                                owed.append(frd[j])
                            if u:
                                turn(u - 1, ends)
                            u += 1
                    turn(u - 1, ends)
                    assert not owed

                hb = ff_space(T)[2]
                assert not owed
                with pe.Fori(0, 2) as it:
                    c.begin(it, (hb_done, SLOTS * T), (narrow_summed, narrow_per_pass(L)),
                            *[(lnd[j], 32) for j in range(SLOTS)])
                    units(SLOTS, narrow_ends(SLOTS * T, narrow_per_pass(L)))
                    c.end(2)
                units(3, narrow_ends(3 * T, narrow_tail(L)[0]))
                pe.wait_ge(ff_ready, c.up(ff_ready, 11 * T))
                for s, (n, kb) in enumerate(DOWN):
                    j = (s + 3) % SLOTS
                    pe.wait_ge(lnd[j], c.up(lnd[j], 32))
                    kn = min(8, FFC - 8 * kb)
                    for t in range(T):
                        bank = t if T == 4 else 2 * n + t
                        if T == 4 and n and kb == 0:
                            pe.wait_ge(y_copied, c.up(y_copied))
                        for k in range(kn):
                            mm = pe.matmul(psum[:, bank, :], ffT[:, 8 * kb + k, t * P:(t + 1) * P], ring[j][:, k, :],
                                           start=(kb == 0 and k == 0), stop=(kb == 2 and k == kn - 1))
                            if k < kn - 1:
                                tag(mm)
                        if kb == 2:
                            mm.then_inc(down_done, 1)
                        else:
                            tag(mm)
                    owed.append(frd[j])
                if L >= 2:
                    pe.wait_ge(y_copied, c.up(y_copied, 4))
                pay(6)

            def route():
                pe.wait_ge(router_in, c.up(router_in, 48))
                for t in range(TX):
                    for k in range(KC):
                        mm = pe.matmul(psum[:, 6, t * E_:(t + 1) * E_], hT[:, k, t * P:(t + 1) * P], router[:, k, :],
                                       start=(k == 0), stop=(k == KC - 1))
                        if k < KC - 1:
                            tag(mm)
                mm.then_inc(logits, 1)
                pe.wait_ge(selected, c.up(selected))
                sel = [rt[:, SEL, t, :] for t in range(TX)]
                pe.matmul(psum[:, 7, 0:E_], tri[:, 3, :], sel[0], start=True, stop=True)
                pe.matmul(psum[:, 7, E_:2 * E_], ones[:, :], sel[0], start=True, stop=False)
                pe.matmul(psum[:, 7, E_:2 * E_], tri[:, 3, :], sel[1], start=False, stop=True)
                pe.matmul(psum[:, 7, 2 * E_:3 * E_], ones[:, :], sel[0], start=True, stop=False)
                pe.matmul(psum[:, 7, 2 * E_:3 * E_], ones[:, :], sel[1], start=False, stop=True).then_inc(positions, 1)

            def gather():
                pe.wait_ge(picked, c.up(picked))
                for f in range(KC):
                    for t in range(TX):
                        mm = pe.matmul(psum[:, 6 + f // 4, (f % 4) * P:(f % 4 + 1) * P],
                                       xn[:, t, f * P:(f + 1) * P], pick[:, t, :], start=(t == 0), stop=(t == TX - 1))
                        if f == 0 and t == 0:
                            tag(mm)
                mm.then_inc(gathered, 1)

            def turn_pick():
                for t in range(TX):
                    tr = transpose(psum[:, 5, t * P:(t + 1) * P], pick_w[:, t, :])
                tr.then_inc(pick_turned, 1)

            def moe(batch):
                narrow = narrow_per_pass(1) if batch == 0 else 0
                ends = narrow_ends(14, narrow)
                gather()
                turn_pick()
                pe.wait_ge(ex_act, c.up(ex_act))
                pe.wait_ge(ex_dve, c.up(ex_dve))
                with pe.Fori(0, E_) as e:
                    c.begin(e, (narrow_summed, narrow), (picked, 1), (ex_act, 1), (ex_dve, 1), (hb_done_e, 14),
                            (ff_ready_e, 14), (ex_y_copied, 1), (pick_wT_ready, 1), *[(landed[j], 96) for j in range(7)])

                    def turn(g):
                        pe.wait_ge(hb_done_e, c.up(hb_done_e))
                        if g == 1:
                            pe.wait_ge(pick_wT_ready, c.up(pick_wT_ready))
                        if g:
                            narrow_columns(2, ends[g - 1], 4 + g % 2)
                        for q in range(2):
                            tr = transpose(psum[:, 4 + g % 2, q * P:(q + 1) * P], ex_hb[:, g % 2, q * P:(q + 1) * P])
                            if q == 0:
                                tag(tr)
                        tr.then_inc(hb_turned_e, 1)

                    for s, (kind, g) in enumerate(MOE_ORDER):
                        j = s % 7
                        if kind == "gu":
                            pe.wait_ge(landed[j], c.up(landed[j], 32))
                            for k in range(KC):
                                mm = pe.matmul(psum[:, g % 2, :], ex_hT[:, k, :], slot_k512[j][:, k, :],
                                               start=(k == 0), stop=(k == KC - 1))
                                if k == 0:
                                    tag(mm)
                            mm.then_inc(gu_done_e, 1)
                            owed.append(freed[j])
                            if g:
                                turn(g - 1)
                        else:
                            if g == 5:
                                gather()
                            if g == 6:
                                turn(13)
                            pe.wait_ge(ff_ready_e, c.up(ff_ready_e, 2))
                            pe.wait_ge(landed[j], c.up(landed[j], 32))
                            for k in range(4):
                                for n in range(2):
                                    mm = pe.matmul(psum[:, 2 + n, :], ex_ff[:, (2 * g + k // 2) % 4, k % 2, :],
                                                   slot_k1024[j][:, k, n * 512:(n + 1) * 512],
                                                   start=(g == 0 and k == 0), stop=(g == 6 and k == 3))
                                    if k == 0 and n == 0:
                                        tag(mm)
                            if g == 6:
                                mm.then_inc(ex_y_done, 1)
                            owed.append(freed[j])
                    turn_pick()
                    pe.wait_ge(ex_act, c.up(ex_act))
                    pe.wait_ge(ex_dve, c.up(ex_dve))
                    pe.wait_ge(ex_y_copied, c.up(ex_y_copied))
                    for t in range(TX):
                        for n in range(2):
                            bank = (6, 2)[t] + n
                            mm = pe.matmul(psum[:, bank, :], pick_wT[:, t * P:(t + 1) * P], ex_y[:, n * 512:(n + 1) * 512],
                                           start=True, stop=True)
                            if n == 0:
                                tag(mm)
                        mm.then_inc(scattered, 1)
                    c.end(E_)
                pe.wait_ge(pick_wT_ready, c.up(pick_wT_ready))

            c.up(narrow_summed)
            pe.wait_ge(consts_in, CONSTS)
            for n, (height, lo) in enumerate(PACKS):
                tr = transpose(psum[:, 6, lo:lo + height], packs[0:height, n, :], height)
            for n in range(2 * CC):
                tr = transpose(psum[:, 7, n * TAPS:(n + 1) * TAPS], conv_raw[0:TAPS, n * P:(n + 1) * P], TAPS)
            tr.then_inc(packs_turned, 1)
            pe.wait_ge(cond_ready, 1)
            pe.wait_ge(ones_set, 1)
            mods(0)
            pe.wait_ge(late_in, LATE)
            for L in stages:
                T = T_IN[L]
                if L < 2:
                    spread(6, diag1)
                norm_turn(T)
                if L < 2:
                    pe.wait_ge(gate_ready, c.up(gate_ready))
                    mixer1(L)
                else:
                    mixer2(L)
                    for _ in range(T_OUT[L] // 2):
                        spread(6, diag2)
                        pe.wait_ge(gate_ready, c.up(gate_ready))
                if L < 2:
                    pe.wait_ge(mix_ready, c.up(mix_ready))
                out_proj(L, T_OUT[L])
                T = T_OUT[L]
                if L >= 2:
                    pe.wait_ge(y_copied, c.up(y_copied, 2 * T))
                    pay(0)
                norm_turn(T)
                dg = diag1 if L == 0 else diag_moe if L == 1 else diag2
                for _ in range(1 if L < 2 else T // 2):
                    spread(6, dg)
                    pe.wait_ge(gate_ready, c.up(gate_ready))
                if L == 1:
                    route()
                    moe(0)
                    over = pe.value_load(flag[0:1, 0:1], min_val=0, max_val=1)
                    with pe.If(over > 0):
                        moe(1)
                else:
                    ffn(L, T)

        SS, RS = 0, 4
        BN, AGG, VR = 8, 14, 18
        PC_, CC_ = 20, 22
        junk = mixT[:, 0:2, :].rearrange("p a b -> p (a b)")

        def shift_col(L, i, k, s):
            return modcol[:, L % 2, 24 * i + k, cond_of(L, s):cond_of(L, s) + 1]

        @block.scalar
        def _(act):
            c = Count()

            def link(ins, sem=None):
                sem = sem or act_link
                ins.then_inc(sem, 1)
                act.wait_ge(sem, c.up(sem))

            def copy_rows(M):
                if not MOD_BLOCKS[M]:
                    return
                with act.Fori(0, MOD_BLOCKS[M] // SLOTS) as it:
                    c.begin(it, (rows_ready, SLOTS))
                    for j in range(SLOTS):
                        act.wait_ge(rows_ready, c.up(rows_ready))
                        act.activation(rows[:, j % 2, :], psum[0:3, j % 2, :], ACT.Copy).then_inc(rows_copied, 1)
                    c.end(MOD_BLOCKS[M] // SLOTS)

            def copy_narrow(M, blocks, bank, base):
                s0, ns = streams_of(M)
                for i, b in enumerate(blocks):
                    lo = GU + 2 * i * ns
                    n = base + 2 * b
                    to = modcol[:, M % 2, n:n + 2, s0:s0 + ns] if isinstance(n, int) else \
                        modcol[:, M % 2, bass.ds(n, 2), s0:s0 + ns]
                    act.activation(to,
                                   psum[:, bank, lo:lo + 2 * ns].rearrange("p (q s) -> p q s", q=2), ACT.Copy)\
                        .then_inc(narrow_copied, 1)

            def copy_gate(s, first_bank=6):
                act.wait_ge(gate_spread, c.up(gate_spread))
                for h in range(2):
                    ins = act.activation(gate_bc[:, s, h * 512:(h + 1) * 512], psum[:, first_bank + h, :], ACT.Copy)
                ins.then_inc(gate_ready, 1)

            def deviations(T):
                act.activation(st[:, RS:RS + T], st[:, SS:SS + T], ACT.Sqrt, bias=eps[:, :], scale=1.0 / D)\
                    .then_inc(root_ready, 1)

            def squares(T, junk_free=False):
                if not junk_free:
                    act.wait_ge(x_ready, c.up(x_ready, T))
                for t in range(T):
                    if junk_free:
                        act.wait_ge(x_ready, c.up(x_ready))
                    act.activation(junk, x[:, t, :], ACT.Square, accum_out=st[:, SS + t:SS + t + 1]).then_inc(ss_ready, 1)
                    act.wait_ge(ss_ready, c.up(ss_ready))
                deviations(T)

            def norm_copy(L, i, T):
                if i == 0:
                    act.wait_ge(mods_ready, c.up(mods_ready))
                for t in range(T):
                    act.wait_ge(xn_turned, c.up(xn_turned))
                    s = t // TX if L >= 2 else 0
                    for k in range(KC // 2, KC):
                        ins = act.activation(hT[:, k, t * P:(t + 1) * P], psum[:, 5, (k - 4) * P:(k - 3) * P],
                                             ACT.Identity, bias=shift_col(L, i, k, s), scale=acol[:, i, s, k:k + 1])
                    ins.then_inc(hT_act, 1)

            def mixer1(L):
                act.wait_ge(proj, c.up(proj, 2))
                act.activation(sig[:, 0:2, :].rearrange("p c t -> p (c t)"), psum[:, 2, :], ACT.Sigmoid)
                act.activation(sig[:, 2, :], psum[:, 3, 0:SEQ], ACT.Sigmoid).then_inc(glu_sig, 1)
                for t in range(TX):
                    act.wait_ge(pool_in, c.up(pool_in))
                    ins = act.activation(pool_tok[:, t, :], psum[:, 6 + t, 0:POOL_W], ACT.Copy)
                ins.then_inc(act_copied, 1)
                act.wait_ge(var_ready, c.up(var_ready, 2))
                act.activation(st[:, VR:VR + TX], st[:, AGG + 1:AGG + 2 * TX:2], ACT.Sqrt, bias=eps[:, :])\
                    .then_inc(root_ready, 1)
                act.wait_ge(proj, c.up(proj, 3))
                act.activation(uT[:, 0:2, :].rearrange("p c t -> p (c t)"), psum[:, 0, :], ACT.Copy)
                act.activation(uT[:, 2, :], psum[:, 1, 0:SEQ], ACT.Copy).then_inc(act_copied, 1)
                act.wait_ge(sgu_turned, c.up(sgu_turned))
                act.activation(sgu_wT[:, 0:4, :].rearrange("p h q -> p (h q)"), psum[:, 2, :], ACT.Copy)
                act.activation(sgu_wT[:, 4:6, :].rearrange("p h q -> p (h q)"), psum[:, 3, 0:2 * P], ACT.Copy)\
                    .then_inc(act_copied, 1)
                act.wait_ge(pool_diff, c.up(pool_diff))
                for j in range(2):
                    for h in range(2):
                        ins = act.activation(diffT[64 * h:64 * h + 64, j, :],
                                             psum[64 * h:64 * h + 64, 6 + j, h * SEQ:(h + 1) * SEQ], ACT.Copy)
                ins.then_inc(diff_copied, 1)
                act.wait_ge(pool_out, c.up(pool_out))
                for j in range(2):
                    act.activation(mixT[:, j, 0:SEQ], psum[:, 6 + j, 0:SEQ], ACT.Copy,
                                   scale=cols[:, 96 + 2 * L + j:97 + 2 * L + j])
                if L + 1 <= max(stages):
                    copy_rows(L + 1)
                act.wait_ge(conv_centred, c.up(conv_centred))
                act.activation(conv_sq, conv_y, ACT.Square).then_inc(conv_squared, 1)
                act.wait_ge(conv_ssum, c.up(conv_ssum))
                act.activation(lnw[:, 1, :], psum[:, 1, 0:SEQ], ACT.Sqrt, bias=eps[:, :], scale=1.0 / CONV_W)\
                    .then_inc(root_ready, 1)
                act.wait_ge(conv_normed, c.up(conv_normed))
                for ch in range(CC):
                    g, b = 96 + 10 + 3 * L + ch, 96 + 16 + 3 * L + ch
                    ins = act.activation(mixT[:, 2 + ch, 0:SEQ], conv_y[:, ch, :], ACT.Silu,
                                         bias=cols[:, b:b + 1], scale=cols[:, g:g + 1])
                ins.then_inc(mix_ready, 1)

            def mixer2(L):
                W = T_OUT[L]
                if L == 3:
                    act.wait_ge(bounds_exp_in, c.up(bounds_exp_in))
                    act.activation(bounds, bounds, ACT.Exp).then_inc(bounds_exp, 1)
                for n, (dst, f) in enumerate(((lambda t: lf_tok[:, t, 0, :], ACT.Sigmoid), (lambda t: lf_tok[:, t, 1, :], ACT.Sigmoid),
                                              (lambda t: v_tok[:, t, :], ACT.Copy), (lambda h: qT[:, h, 0:W * P], ACT.Silu),
                                              (lambda t: dqk[:, t, :], ACT.Copy), (lambda t: dvft[:, t, :], ACT.Copy),
                                              (lambda t: g_tok[:, t, :], ACT.Silu))):
                    if n == 6:
                        act.wait_ge(forget_ready, c.up(forget_ready))
                        act.activation(lf_tok, lf_tok, ACT.Ln).then_inc(log_ready, 1)
                    for t in range(W if n == 6 else 4):
                        act.wait_ge(proj, c.up(proj))
                        to = dst(t)
                        act.activation(to, psum[:, 4 * (n % 2) + t, 0:to.shape[1]], f).then_inc(in_copied, 1)
                if L + 1 <= max(stages):
                    copy_rows(L + 1)
                act.wait_ge(lam_in, c.up(lam_in))
                act.activation(st[:, LAM:LAM + 2], st[:, LAM:LAM + 2], ACT.Exp).then_inc(lam_exp, 1)
                act.wait_ge(dqk_turned, c.up(dqk_turned))
                for ch in range(4):
                    ins = act.activation(dqkT[:, ch, :], psum[:, 4 + ch, :], ACT.Copy)
                ins.then_inc(dqkT_ready, 1)
                for s in range(W // 2):
                    for j in range(2):
                        act.wait_ge(fourier_ps, c.up(fourier_ps))
                        act.activation(fu, psum[:, 0, :], ACT.Copy).then_inc(fourier_sb, 1)
                        act.wait_ge(fourier_ps, c.up(fourier_ps))
                        act.activation(mixT[:, 6 + j, s * SEQ:(s + 1) * SEQ], psum[:, 1, 0:SEQ], ACT.Copy)\
                            .then_inc(fourier_sb, 1)
                units = W * HEADS
                for u in range(units + 2):
                    if u < units:
                        act.wait_ge(attn_max, c.up(attn_max))
                        N = 512 if u // HEADS < TX else SEQ
                        for m in range(2):
                            ins = act.activation(probs[:, m, 0:N], psum[:, 2 * (u % 2) + m, 0:N], ACT.Exp,
                                                 bias=st[:, NMX + m:NMX + m + 1], scale=ATT_SCALE,
                                                 accum_out=st[:, DEN + m:DEN + m + 1])
                        ins.then_inc(attn_exp, 1)
                    if 0 <= u - 1 < units:
                        act.wait_ge(attn_wT, c.up(attn_wT))
                        n = 4 if (u - 1) // HEADS < TX else 2
                        act.activation(wT[:, (u - 1) % 2, 0:n, :].rearrange("p k q -> p (k q)"),
                                       psum[:, 4 + (u - 1) % 2, 0:n * P], ACT.Copy).then_inc(attn_wT_sb, 1)
                    if u >= 2 and (u - 2) % HEADS == HEADS - 1:
                        t = (u - 2) // HEADS
                        act.wait_ge(attn_o, c.up(attn_o, HEADS))
                        act.activation(od_tok[:, t, :], psum[:, 6 + t % 2, 0:256], ACT.Copy).then_inc(attn_o_sb, 1)

                def heads_out(n, width, lo):
                    act.wait_ge(head_ss, c.up(head_ss))
                    act.activation(st[:, HS:HS + 4 * W], st[:, HS:HS + 4 * W], ACT.Sqrt, bias=eps[:, :], scale=1.0 / width)\
                        .then_inc(root_ready, 1)
                    for t in range(W):
                        act.wait_ge(out_turned, c.up(out_turned))
                        act.activation(mixT[:, lo:lo + n, t * P:(t + 1) * P],
                                       psum[:, 4 + t % 2, 0:n * P].rearrange("p (c t) -> p c t", c=n), ACT.Copy)\
                            .then_inc(out_copied, 1)
                heads_out(2, 64, 4)
                for i, (d, t) in enumerate(SCAN):
                    act.wait_ge(scan_in, c.up(scan_in))
                    if i:
                        act.wait_ge(scan_kd, c.up(scan_kd))
                        if SCAN[i - 1][1] < W:
                            act.wait_ge(level_qk, c.up(level_qk, LEVELS))
                    if i >= 2:
                        act.wait_ge(scan_done, c.up(scan_done))
                    act.activation(k_out, psum[:, 1, :], ACT.Exp)
                    if t < W:
                        act.activation(b_T, psum[:, 0, :], ACT.Copy)
                        act.activation(k_T, psum[:, 2, :], ACT.Copy)
                    act.activation(b_exp[i % 2], psum[:, 0, :], ACT.Exp).then_inc(scan_sb, 1)
                    if t < W:
                        for lv in range(LEVELS):
                            act.wait_ge(level_arg, c.up(level_arg))
                            act.activation(decay[:, lv % 2, :], decay[:, lv % 2, :], ACT.Exp).then_inc(level_exp, 1)
                c.up(scan_kd)
                c.up(scan_done, 2)
                if SCAN[-1][1] < W:
                    c.up(level_qk, LEVELS)
                heads_out(4, P, 0)

            def ffn(L, T):
                ffT, sg, _ = ff_space(T)

                def units(blocks, b0, ends=(), base=0):
                    def turned(u):
                        act.wait_ge(hb_turned, c.up(hb_turned))
                        if u and ends:
                            copy_narrow(L + 1, ends[u - 1], 4 + u % 2, base)
                        dst = ffT[:, bass.ds(b0 * 2 + 2 * (u // T), 2), (u % T) * P:(u % T + 1) * P]
                        act.activation(dst, psum[:, 4 + u % 2, 0:GU].rearrange("p (q t) -> p q t", q=2), ACT.Copy)\
                            .then_inc(ff_ready, 1)
                    for u in range(blocks * T):
                        act.wait_ge(gu_done, c.up(gu_done))
                        act.activation(sg[:, u % 2, :], psum[:, u % 4, 0:GU], ACT.Silu).then_inc(silu_done, 1)
                        if u:
                            turned(u - 1)
                    turned(blocks * T - 1)

                with act.Fori(0, 2) as it:
                    c.begin(it, (gu_done, SLOTS * T), (hb_turned, SLOTS * T))
                    n = narrow_per_pass(L)
                    base = it * (2 * n) + 2 * narrow_first(L + 1) if n else 0
                    units(SLOTS, it * SLOTS, narrow_ends(SLOTS * T, n), base)
                    c.end(2)
                tail, before = narrow_tail(L)
                base = 2 * narrow_first(L + 1) + 2 * before if tail else 0
                units(3, 2 * SLOTS, narrow_ends(3 * T, tail), base)

            def post_norm(sem, L, T):
                for n in range(2):
                    for t in range(T):
                        act.wait_ge(sem, c.up(sem))
                        bank = post_bank(sem, n, t, T)
                        act.activation(ybuf[:, t, n * 512:(n + 1) * 512], psum[:, bank, :], ACT.Copy)\
                            .then_inc(y_copied, 1)
                act.wait_ge(y_copied, c.up(y_copied, 2 * T))
                for t in range(T):
                    act.activation(junk, ybuf[:, t, :], ACT.Square, accum_out=st[:, SS + t:SS + t + 1])\
                        .then_inc(ss_ready, 1)
                    act.wait_ge(ss_ready, c.up(ss_ready))
                deviations(T)

            def moe(batch):
                narrow = narrow_per_pass(1) if batch == 0 else 0
                ends = narrow_ends(14, narrow)

                def upper_half():
                    act.wait_ge(gathered, c.up(gathered))
                    for k in range(KC // 2, KC):
                        ins = act.activation(ex_hT[:, k, :], psum[:, 7, (k - 4) * P:(k - 3) * P],
                                             ACT.Identity, bias=shift_col(1, 1, k, 0), scale=acol[:, 1, 0, k:k + 1])
                    ins.then_inc(ex_act, 1)
                upper_half()
                with act.Fori(0, E_) as e:
                    c.begin(e, (gathered, 1), (gu_done_e, 14), (hb_turned_e, 14), (ex_y_done, 1))

                    def turned(g):
                        act.wait_ge(hb_turned_e, c.up(hb_turned_e))
                        if g:
                            copy_narrow(2, ends[g - 1], 4 + g % 2, e * (2 * narrow) + 2 * narrow_first(2))
                        act.activation(ex_ff[:, g % 4, :, :].rearrange("p q t -> p (q t)"), psum[:, 4 + g % 2, 0:GU], ACT.Copy)\
                            .then_inc(ff_ready_e, 1)
                    for g in range(14):
                        act.wait_ge(gu_done_e, c.up(gu_done_e))
                        act.activation(ex_sg[:, g % 2, :], psum[:, g % 2, 0:GU], ACT.Silu).then_inc(silu_done_e, 1)
                        if g:
                            turned(g - 1)
                    upper_half()
                    turned(13)
                    act.wait_ge(ex_y_done, c.up(ex_y_done))
                    for n in range(2):
                        ins = act.activation(ex_y[:, n * 512:(n + 1) * 512], psum[:, 2 + n, :], ACT.Copy)
                    ins.then_inc(ex_y_copied, 1)
                    c.end(E_)

            act.wait_ge(consts_in, CONSTS)
            act.activation(cond[:, :, :], cond_raw[:, :, :].rearrange("p n k -> p k n"), ACT.Silu).then_inc(cond_ready, 1)
            act.wait_ge(ones_set, 1)
            copy_rows(0)
            act.wait_ge(late_in, LATE)
            act.wait_ge(cols_ready, 1)
            for L in stages:
                T = T_IN[L]
                squares(T, L == 3)
                if L < 2:
                    copy_gate(0)
                norm_copy(L, 0, T)
                if L < 2:
                    mixer1(L)
                else:
                    mixer2(L)
                    for s in range(T_OUT[L] // 2):
                        copy_gate(s)
                T = T_OUT[L]
                if L >= 2:
                    post_norm(w_out_done, L, T)
                else:
                    c.up(w_out_done, 2 * T)
                squares(T, L >= 2)
                norm_copy(L, 1, T)
                for s in range(1 if L < 2 else T // 2):
                    copy_gate(s)
                if L == 1:
                    act.wait_ge(route_exp_in, c.up(route_exp_in))
                    act.activation(rt[:, EXPD, :, 0], rt[:, DIFF, :, 0], ACT.Exp).then_inc(route_exp, 1)
                    moe(0)
                    act.wait_ge(routed, 1)
                    over = act.value_load(flag[0:1, 0:1], min_val=0, max_val=1)
                    with act.If(over > 0):
                        moe(1)
                else:
                    ffn(L, T)
                    if L >= 2:
                        post_norm(down_done, L, T)
                    else:
                        c.up(down_done, 2 * T)
                if L == LAST1:
                    squares(TX)

        @block.vector
        def _(dve):
            c = Count()
            TT = dve.tensor_tensor
            TS = dve.tensor_scalar
            STT = dve.scalar_tensor_tensor

            def link(ins, sem=None):
                sem = sem or dve_link
                ins.then_inc(sem, 1)
                dve.wait_ge(sem, c.up(sem))

            def mods_to_columns(L):
                n = 4 * MOD_BLOCKS[L]
                if not n:
                    return
                dve.wait_ge(mods_turned, c.up(mods_turned, MOD_BLOCKS[L] // SLOTS))
                bias = cols[:, 118 + 48 * L:118 + 48 * L + n].rearrange("p (n o) -> p n o", o=1)
                link(TT(modcol[:, L % 2, 0:n, :], psum[:, 3, 0:3 * n].rearrange("p (n s) -> p n s", s=3),
                        bias.to_broadcast((P, n, 3)), ALU.add))

            def narrow_bias(M):
                dve.wait_ge(narrow_copied, c.up(narrow_copied, NARROW_ALL - narrow_first(M)))
                lo, (s0, ns) = 4 * MOD_BLOCKS[M], streams_of(M)
                m = modcol[:, M % 2, lo:MODC, s0:s0 + ns]
                bias = cols[:, 118 + 48 * M + lo:118 + 48 * (M + 1)].rearrange("p (n o) -> p n o", o=1)
                link(TT(m, m, bias.to_broadcast((P, MODC - lo, ns)), ALU.add))

            def narrow_counts(blocks):
                return [(narrow_spread, blocks), (narrow_in[0], 16 * blocks), (narrow_in[1], 16 * blocks),
                        (narrow_link, 6 * blocks), (narrow_used, blocks), (narrow_summed, blocks)]

            def narrow_halves(M, first, n):
                s0, ns = streams_of(M)
                for half in range(first, first + n):
                    b, h = half // 2, half % 2
                    if h == 0:
                        dve.wait_ge(narrow_spread, c.at(narrow_spread) + 1)
                        c.up(narrow_spread)
                    dve.wait_ge(narrow_in[h], c.up(narrow_in[h], 16))
                    w = narrow_buf(M, h)
                    for k in range(4):
                        for s in range(ns):
                            acc, f = mod_sum[:, b % 2, s, :], cond[:, 4 * h + k, s0 + s:s0 + s + 1]
                            if h == 0 and k == 0:
                                ins = TS(acc, w[:, k, :], f, None, ALU.mult)
                            else:
                                ins = STT(acc, w[:, k, :], f, acc, ALU.mult, ALU.add)
                        if k < 3:
                            link(ins, narrow_link)
                    link(ins, narrow_summed if h else narrow_used)

            def layer_columns(L):
                for i in range(2):
                    for s in range(1 if L < 2 else 2):
                        m = modcol[:, L % 2, 24 * i:24 * i + 24, cond_of(L, s)]
                        g = gain_cols(L, i)
                        STT(acol[:, i, s, :], m[:, 8:16], 1.0, g, ALU.add, ALU.mult)
                        if L < 2:
                            ins = dve.tensor_copy(gcol[:, i, s, :], m[:, 16:24])
                        else:
                            ins = TT(gcol[:, i, s, :], m[:, 16:24], post_cols(L, i), ALU.mult)
                ins.then_inc(mods_ready, 1)
                dve.wait_ge(mods_ready, c.up(mods_ready))

            diagonals = []

            def diagonal(dst, i, s):
                if diagonals:
                    dve.wait_ge(gate_spread, c.up(gate_spread))
                diagonals.append(i)
                g = gcol[:, i, s, :].rearrange("p (k o) -> p k o", o=1)
                TT(dst, ident[:, :].rearrange("p (o f) -> p o f", o=1).to_broadcast((P, KC, P)),
                   g.to_broadcast((P, KC, P)), ALU.mult).then_inc(diag_ready, 1)

            def inverse_dev(T):
                dve.wait_ge(root_ready, c.up(root_ready))
                link(dve.reciprocal(st[:, RS:RS + T], st[:, RS:RS + T]))

            def norm(L, i, T):
                def normed(t):
                    TS(xn[:, t % 2, :], x[:, t, :], st[:, RS + t:RS + t + 1], None, ALU.mult).then_inc(xn_ready, 1)
                inverse_dev(T)
                normed(0)
                for t in range(T):
                    if t + 1 < T and t + 1 < 2:
                        normed(t + 1)
                    dve.wait_ge(xn_turned, c.up(xn_turned))
                    s = t // TX if L >= 2 else 0
                    for k in range(KC // 2):
                        ins = TS(hT[:, k, t * P:(t + 1) * P], psum[:, 4, k * P:(k + 1) * P],
                                 acol[:, i, s, k:k + 1], shift_col(L, i, k, s), ALU.mult, ALU.add)
                    ins.then_inc(hT_dve, 1)
                    if 2 <= t + 2 < T:
                        normed(t + 2)

            def mixer1(L):
                dve.wait_ge(proj, c.up(proj, 2))
                dve.wait_ge(glu_sig, c.up(glu_sig))
                dve.memset(glu[:, :, 0:PAD], 0.0)
                dve.memset(glu[:, :, PAD + SEQ:], 0.0)
                TT(glu[:, 0:2, PAD:PAD + SEQ], psum[:, 0, :].rearrange("p (c t) -> p c t", c=2), sig[:, 0:2, :], ALU.mult)
                TT(glu[:, 2, PAD:PAD + SEQ], psum[:, 1, 0:SEQ], sig[:, 2, :], ALU.mult).then_inc(glu_done, 1)
                for t in range(TX):
                    dve.wait_ge(proj, c.up(proj))
                    link(dve.bn_stats(st[:, BN:BN + 6], psum[:, 4 + t, 0:SGU_W]))
                    dve.bn_aggr(st[:, AGG + 2 * t:AGG + 2 * t + 2], st[:, BN:BN + 6]).then_inc(var_ready, 1)
                    dve.wait_ge(var_ready, c.up(var_ready))
                dve.wait_ge(root_ready, c.up(root_ready))
                link(dve.reciprocal(st[:, VR:VR + TX], st[:, VR:VR + TX]))
                for t in range(TX):
                    v = psum[:, 4 + t, 0:SGU_W]
                    link(TS(v_n[:, t, :], v, st[:, AGG + 2 * t:AGG + 2 * t + 1], st[:, VR + t:VR + t + 1],
                            ALU.subtract, ALU.mult))
                    link(TT(v_n[:, t, :], v_n[:, t, :], sgu_ln[:, 2 * L, :], ALU.mult))
                    ins = TT(v_n[:, t, :], v_n[:, t, :], sgu_ln[:, 2 * L + 1, :], ALU.add)
                ins.then_inc(v_normed, 1)
                c.up(proj)
                dve.wait_ge(glu_done, c.up(glu_done))
                for k in range(TAPS):
                    for ch in range(CC):
                        g = glu[:, ch, k:k + SEQ]
                        w = conv_cols[:, L * CC + ch, k:k + 1]
                        if k == 0:
                            ins = TS(conv_y[:, ch, :], g, w, cols[:, 100 + 3 * L + ch:101 + 3 * L + ch], ALU.mult, ALU.add)
                        else:
                            dve.wait_ge(dve_link, c.at(dve_link) - (CC - 1))
                            ins = STT(conv_y[:, ch, :], g, w, conv_y[:, ch, :], ALU.mult, ALU.add)
                        ins.then_inc(conv_done if (k, ch) == (TAPS - 1, CC - 1) else dve_link, 1)
                        if (k, ch) != (TAPS - 1, CC - 1):
                            c.up(dve_link)
                dve.wait_ge(act_copied, c.up(act_copied, 3))
                dve.wait_ge(sgu_mixed, c.up(sgu_mixed))
                for n in range(TX * CC):
                    t, j = n // CC, n % CC
                    for h in range(2):
                        r = slice(64 * h, 64 * h + 64)
                        lo = (n % 2) * SEQ + h * P
                        ins = TT(mixT[r, 5 + j, t * P:(t + 1) * P], uT[r, j, t * P:(t + 1) * P],
                                 psum[r, SGU_BANK[n // 2], lo:lo + P], ALU.mult)
                if L + 1 <= max(stages):
                    mods_to_columns(L + 1)
                dve.wait_ge(conv_done, c.up(conv_done))
                dve.wait_ge(conv_sum, c.up(conv_sum))
                link(TS(lnw[:, 0, :], psum[:, 0, 0:SEQ], 1.0 / CONV_W, None, ALU.mult))

                def rows_of(i):
                    return lnw[:, i, :].rearrange("p (o t) -> p o t", o=1).to_broadcast((P, CC, SEQ))
                TT(conv_y, conv_y, rows_of(0), ALU.subtract).then_inc(conv_centred, 1)
                dve.wait_ge(conv_centred, c.up(conv_centred))
                dve.wait_ge(root_ready, c.up(root_ready))
                link(dve.reciprocal(lnw[:, 1, :], lnw[:, 1, :]))
                TT(conv_y, conv_y, rows_of(1), ALU.mult).then_inc(conv_normed, 1)

            def gated_add(sem, T):
                for n in range(2):
                    for t in range(T):
                        dve.wait_ge(sem, c.up(sem))
                        link(TT(prod, psum[:, (2, 3, 6, 7)[2 * n + t] if sem is w_out_done else 2 * n + t, :],
                                gate_bc[:, 0, n * 512:(n + 1) * 512], ALU.mult))
                        ins = TT(x[:, t, n * 512:(n + 1) * 512], x[:, t, n * 512:(n + 1) * 512], prod, ALU.add)
                        if n:
                            ins.then_inc(x_ready, 1)
                            dve.wait_ge(x_ready, c.up(x_ready))
                        else:
                            link(ins)

            def mixer2(L):
                W = T_OUT[L]
                X = lambda ap: ap.rearrange("p (o n) -> p o n", o=1)
                if L == 3:
                    dve.wait_ge(params2_in, PAR2[L])
                    lo, hi = bounds[:, :, 0, :], bounds[:, :, 1, :]
                    link(TT(bound_tmp, lo, hi, ALU.max))
                    link(TT(lo, lo, bound_tmp, ALU.subtract))
                    TT(hi, hi, bound_tmp, ALU.subtract).then_inc(bounds_exp_in, 1)
                    dve.wait_ge(bounds_exp, c.up(bounds_exp))
                    link(TT(bound_tmp, lo, hi, ALU.add))
                    link(dve.reciprocal(bound_tmp, bound_tmp))
                    link(TT(hi, hi, bound_tmp, ALU.mult))
                    link(TS(lo, hi, -1.0, 1.0, ALU.mult, ALU.add))
                for d in range(2):
                    for t in range(4):
                        dve.wait_ge(in_copied, c.up(in_copied))
                        f = lf_tok[:, t, d, :]
                        if L == 3:
                            link(TT(f, f, bounds[:, d, 0, :], ALU.mult))
                            link(TT(f, f, bounds[:, d, 1, :], ALU.add))
                        TS(k_tok[:, t, d, :], f, -1.0, 1.0, ALU.mult, ALU.add)
                        ins = TS(f, f, LN_FLOOR, None, ALU.max)
                ins.then_inc(forget_ready, 1)
                if L + 1 <= max(stages):
                    mods_to_columns(L + 1)
                dve.wait_ge(params2_in, PAR2[L])
                pairs = lam4.rearrange("p (a b d) -> p a b d", a=2, b=2)
                dve.wait_ge(in_copied, c.up(in_copied, 12))
                tmp = rope_tmp[:, 0, 0:64].rearrange("p (a d) -> p a d", a=2)
                c.up(in_copied, 4 + W)
                dve.wait_ge(in_copied, c.at(in_copied))
                link(TT(tmp, pairs[:, :, 0, :], pairs[:, :, 1, :], ALU.mult))
                dve.reduce_sum(st[:, LAM:LAM + 2], tmp, AX_X).then_inc(lam_in, 1)
                link(TS(subln, subln, 1.0 - LAM_INIT[L - 2], None, ALU.mult))
                dve.wait_ge(lam_exp, c.up(lam_exp))
                link(TT(st[:, LAM + 2:LAM + 3], st[:, LAM + 1:LAM + 2], st[:, LAM:LAM + 1], ALU.subtract))
                link(TS(st[:, LAM + 2:LAM + 3], st[:, LAM + 2:LAM + 3], -LAM_INIT[L - 2], None, ALU.add))
                for t in range(TX):
                    r1, r2 = rope_tmp[:, 0, :], rope_tmp[:, 1, :]
                    v5 = lambda ap: ap.rearrange("p (g a h j) -> p g a h j", a=2, h=2, j=8)
                    cos = X(rope[:, t, 0, :]).to_broadcast((P, 16, 32))
                    TT(r1.rearrange("p (g n) -> p g n", g=16), dqk[:, t, :].rearrange("p (g n) -> p g n", g=16), cos, ALU.mult)
                    for h in range(2):
                        sin = rope[:, t, 1, :].rearrange("p (o a h j) -> p o a h j", o=1, a=2, h=2)[:, :, :, h, :]\
                            .to_broadcast((P, 16, 2, 8))
                        ins = TT(v5(r2)[:, :, :, h, :], v5(dqk[:, t, :])[:, :, :, 1 - h, :], sin, ALU.mult)
                    link(ins)
                    ins = TT(dqk[:, t, :], r1, r2, ALU.add)
                    if t == 0:
                        link(ins)
                ins.then_inc(roped, 1)
                for u in range(W * HEADS):
                    N = 512 if u // HEADS < TX else SEQ
                    dve.wait_ge(attn_scores, c.up(attn_scores))
                    link(dve.reduce_max(st[:, MX:MX + 2], psum[:, 2 * (u % 2):2 * (u % 2) + 2, 0:N], AX_X))
                    TS(st[:, NMX:NMX + 2], st[:, MX:MX + 2], -ATT_SCALE, None, ALU.mult).then_inc(attn_max, 1)
                    dve.wait_ge(attn_exp, c.up(attn_exp))
                    link(dve.reciprocal(st[:, RDEN:RDEN + 2], st[:, DEN:DEN + 2]))
                    link(TT(st[:, RDEN + 1:RDEN + 2], st[:, RDEN + 1:RDEN + 2], st[:, LAM + 2:LAM + 3], ALU.mult))
                    link(TS(weights[:, u % 2, 0:N], probs[:, 0, 0:N], st[:, RDEN:RDEN + 1], None, ALU.mult))
                    STT(weights[:, u % 2, 0:N], probs[:, 1, 0:N], st[:, RDEN + 1:RDEN + 2], weights[:, u % 2, 0:N],
                        ALU.mult, ALU.add).then_inc(attn_w, 1)

                def head_norm(tok, width, gain, times):
                    n = HEADS * width
                    four = lambda ap: ap.rearrange("p (h n) -> p h n", h=HEADS)
                    for t in range(W):
                        tmp = decay[:, t % 2, 0:n]
                        link(TT(tmp, tok[:, t, :], tok[:, t, :], ALU.mult))
                        ins = dve.reduce_sum(st[:, HS + 4 * t:HS + 4 * t + 4], four(tmp), AX_X)
                    ins.then_inc(head_ss, 1)
                    dve.wait_ge(root_ready, c.up(root_ready))
                    link(dve.reciprocal(st[:, HS:HS + 4 * W], st[:, HS:HS + 4 * W]))
                    for t in range(W):
                        r = st[:, HS + 4 * t:HS + 4 * t + 4].rearrange("p (h o) -> p h o", o=1).to_broadcast((P, HEADS, width))
                        o = four(tok[:, t, :])
                        link(TT(o, o, r, ALU.mult))
                        ins = TT(o, o, X(gain).to_broadcast((P, HEADS, width)), ALU.mult)
                        if times is not None:
                            link(ins)
                            ins = TT(tok[:, t, :], tok[:, t, :], times[:, t, :], ALU.mult)
                        ins.then_inc(out_normed, 1)
                dve.wait_ge(attn_o_sb, c.up(attn_o_sb, W))
                head_norm(od_tok, 64, subln, None)

                dve.wait_ge(log_ready, c.up(log_ready))
                dve.memset(qw, 0.0)
                link(dve.memset(kw, 0.0))
                eye = X(ident[:, :]).to_broadcast((P, HEADS, P))
                heads = lambda ap: ap.rearrange("p (h n) -> p h n", h=HEADS)
                seen = set()
                for i, (d, t) in enumerate(SCAN):
                    want = t < W
                    dve.wait_ge(scan_sb, c.up(scan_sb))
                    if want:
                        q = qT[:, :, t * P:(t + 1) * P]

                        def blocks(ap, m):
                            return ap.rearrange("p (n two m) -> p n two m", two=2, m=m)

                        def arg(lv):
                            if lv >= 2:
                                dve.wait_ge(level_qk, c.at(level_qk))
                            m = P >> (lv + 1)
                            b, e = blocks(b_T, m), blocks(decay[:, lv % 2, :], m)
                            n = HG // (2 * m)
                            ref = (b[:, :, 0, m - 1:m] if d == 0 else b[:, :, 1, 0:1]).to_broadcast((P, n, m))
                            to, of = 1 - d, d
                            TT(e[:, :, to, :], b[:, :, to, :], ref, ALU.subtract)
                            TT(e[:, :, of, :], ref, b[:, :, of, :], ALU.subtract).then_inc(level_arg, 1)

                        def decayed(lv):
                            m = P >> (lv + 1)
                            dve.wait_ge(level_exp, c.up(level_exp))
                            e = decay[:, lv % 2, :]
                            to, of = 1 - d, d
                            qb = q.rearrange("p h (n two m) -> p h n two m", two=2, m=m)
                            e5 = e.rearrange("p (h n two m) -> p h n two m", h=HEADS, two=2, m=m)
                            w5 = qw[:, lv % 2, :].rearrange("p (h n two m) -> p h n two m", h=HEADS, two=2, m=m)
                            TT(w5[:, :, :, to, :], qb[:, :, :, to, :], e5[:, :, :, to, :], ALU.mult)
                            TT(blocks(kw[:, lv % 2, :], m)[:, :, of, :], blocks(k_T, m)[:, :, of, :],
                               blocks(e, m)[:, :, of, :], ALU.mult).then_inc(level_qk, 1)
                            c.up(level_qk)

                        def put(lv):
                            dve.wait_ge(level_ps, c.up(level_ps))
                            mask = X(masks[:, d, lv, :]).to_broadcast((P, HEADS, P))
                            dve.copy_predicated(heads(scores[:, d, :]), mask, heads(psum[:, 4 + lv % 2, :])).then_inc(level_put, 1)
                            dve.wait_ge(level_put, c.up(level_put))

                        arg(0)
                        arg(1)
                    TT(k_tok[:, t, d, :], k_tok[:, t, d, :], k_out, ALU.mult).then_inc(scan_kd, 1)
                    if want:
                        TT(heads(q_in), q, heads(b_exp[i % 2]), ALU.mult)
                        dve.wait_ge(level_ps, c.up(level_ps))
                        TT(heads(scores[:, d, :]), heads(psum[:, 6, :]), eye, ALU.mult).then_inc(level_put, 1)
                        dve.wait_ge(level_put, c.up(level_put))
                        for lv in range(LEVELS):
                            decayed(lv)
                            if lv + 2 < LEVELS:
                                arg(lv + 2)
                            if lv:
                                put(lv - 1)
                        put(LEVELS - 1)
                    dve.wait_ge(scan_o, c.up(scan_o))
                    if want:
                        dve.wait_ge(scan_o, c.up(scan_o))
                        if FIRST[t] == d:
                            ins = dve.tensor_copy(o_tok[:, t, :], psum[:, 7, :])
                        else:
                            ins = TT(o_tok[:, t, :], o_tok[:, t, :], psum[:, 7, :], ALU.add)
                    if t != (1, 0)[d]:
                        for h in range(HEADS):
                            if d in seen:
                                edge = h * P + (P - 1 if d == 0 else 0)
                                ins = STT(state[:, d, h, :], state[:, d, h, :], b_exp[i % 2][:, edge:edge + 1],
                                          psum[:, 3, h * P:(h + 1) * P], ALU.mult, ALU.add)
                            else:
                                ins = dve.tensor_copy(state[:, d, h, :], psum[:, 3, h * P:(h + 1) * P])
                    seen.add(d)
                    ins.then_inc(scan_done, 1)
                    dve.wait_ge(scan_done, c.up(scan_done))
                head_norm(o_tok, P, onorm, g_tok)

            def ffn(L, T):
                _, sg, hb = ff_space(T)

                def units(n, plan=()):
                    for u in range(n):
                        dve.wait_ge(silu_done, c.up(silu_done))
                        TT(hb[:, u % 2, :], sg[:, u % 2, :], psum[:, u % 4, GU:2 * GU], ALU.mult).then_inc(hb_done, 1)
                        if plan:
                            narrow_halves(L + 1, sum(plan[:u]), plan[u])
                narrow = narrow_per_pass(L)
                with dve.Fori(0, 2) as it:
                    c.begin(it, (silu_done, SLOTS * T), *narrow_counts(narrow))
                    units(SLOTS * T, narrow_plan(SLOTS * T, narrow))
                    c.end(2)
                units(3 * T, narrow_plan(3 * T, narrow_tail(L)[0]))
                if narrow:
                    narrow_bias(L + 1)

            def post_add(L, T):
                inverse_dev(T)
                for t in range(T):
                    s = t // TX
                    link(STT(ybuf[:, t, :], ybuf[:, t, :], st[:, RS + t:RS + t + 1], gate_bc[:, s, :], ALU.mult, ALU.mult))
                    TT(x[:, t, :], x[:, t, :], ybuf[:, t, :], ALU.add).then_inc(x_ready, 1)
                    dve.wait_ge(x_ready, c.up(x_ready))

            def route():
                R = lambda n: rt[:, n, :, :]
                R0 = lambda n: rt[:, n, :, 0:1]
                dve.wait_ge(logits, c.up(logits))
                dve.wait_ge(router_in, 48)
                bias = router_bias.rearrange("p (o e) -> p o e", o=1).to_broadcast((P, TX, E_))
                link(TT(R(LOGIT), psum[:, 6, 0:TX * E_].rearrange("p (t e) -> p t e", t=TX), bias, ALU.add))
                for t in range(TX):
                    link(dve.max(rt[:, TOP, t, :], rt[:, LOGIT, t, :]))
                for t in range(TX):
                    first, second = rt[:, TOP, t, 0:1], rt[:, TOP, t, 1:2]
                    link(TS(rt[:, EQ1, t, :], rt[:, LOGIT, t, :], first, None, ALU.is_equal))
                    link(cumulate(t, EQ1))
                    link(STT(rt[:, SEL1, t, :], rt[:, CUM, t, :], 1.0, rt[:, EQ1, t, :], ALU.is_equal, ALU.mult))
                    link(STT(rt[:, EQ2, t, :], rt[:, LOGIT, t, :], second, rt[:, SEL1, t, :], ALU.is_equal, ALU.subtract))
                    link(TS(rt[:, EQ2, t, :], rt[:, EQ2, t, :], 0.0, None, ALU.max))
                    link(cumulate(t, EQ2))
                    link(STT(rt[:, SEL2, t, :], rt[:, CUM, t, :], 1.0, rt[:, EQ2, t, :], ALU.is_equal, ALU.mult))
                TT(R(SEL), R(SEL1), R(SEL2), ALU.add).then_inc(selected, 1)
                dve.wait_ge(selected, c.up(selected))
                TT(R0(DIFF), rt[:, TOP, :, 1:2], rt[:, TOP, :, 0:1], ALU.subtract).then_inc(route_exp_in, 1)
                dve.wait_ge(route_exp, c.up(route_exp))
                link(TS(R0(W1), R0(EXPD), 1.0, None, ALU.add))
                link(dve.reciprocal(R0(W1), R0(W1)))
                link(TT(R0(W2), R0(W1), R0(EXPD), ALU.mult))
                for t in range(TX):
                    link(TS(rt[:, COMB, t, :], rt[:, SEL1, t, :], rt[:, W1, t, 0:1], None, ALU.mult))
                    link(STT(rt[:, COMB, t, :], rt[:, SEL2, t, :], rt[:, W2, t, 0:1], rt[:, COMB, t, :], ALU.mult, ALU.add))
                dve.wait_ge(positions, c.up(positions))
                link(STT(R(POS), psum[:, 7, 0:2 * E_].rearrange("p (t e) -> p t e", t=TX), 1.0, R(SEL), ALU.add, ALU.mult))
                link(TS(R(POS), R(POS), -1.0, None, ALU.add))
                link(dve.reduce_max(rt[:, W1, 0, 1:2], psum[:, 7, 2 * E_:3 * E_], AX_X))
                TS(flag[:, :], rt[:, W1, 0, 1:2], float(P), None, ALU.is_gt).then_inc(routed, 1)
                dve.wait_ge(routed, 1)

            def cumulate(t, n):
                return dve.tensor_tensor_scan(rt[:, CUM, t, :], ones[:, 0:E_], rt[:, n, t, :], 0.0, ALU.mult, ALU.add)

            def moe(batch):
                narrow = narrow_per_pass(1) if batch == 0 else 0
                plan = narrow_plan(14, narrow)
                per_token = rt.rearrange("p n t e -> p (n t e)")

                def choose(e):
                    for t in range(TX):
                        at = TX * E_ * POS + E_ * t
                        dve.tensor_copy(st[:, PC_ + t:PC_ + t + 1], per_token[:, bass.ds(e + at, 1)])
                        at = TX * E_ * COMB + E_ * t
                        ins = dve.tensor_copy(st[:, CC_ + t:CC_ + t + 1], per_token[:, bass.ds(e + at, 1)])
                    link(ins, moe_link)
                    for t in range(TX):
                        link(TS(pick[:, t, :], iota[:, batch * P:(batch + 1) * P], st[:, PC_ + t:PC_ + t + 1], None, ALU.is_equal),
                             moe_link)
                    for t in range(TX):
                        ins = TS(pick_w[:, t, :], pick[:, t, :], st[:, CC_ + t:CC_ + t + 1], None, ALU.mult)
                    ins.then_inc(picked, 1)

                def lower_half():
                    dve.wait_ge(gathered, c.up(gathered))
                    for k in range(KC // 2):
                        ins = TS(ex_hT[:, k, :], psum[:, 6, k * P:(k + 1) * P], acol[:, 1, 0, k:k + 1], shift_col(1, 1, k, 0),
                                 ALU.mult, ALU.add)
                    ins.then_inc(ex_dve, 1)

                def copy_pick():
                    dve.wait_ge(pick_turned, c.up(pick_turned))
                    dve.tensor_copy(pick_wT, psum[:, 5, 0:2 * P]).then_inc(pick_wT_ready, 1)

                choose(0)
                lower_half()
                copy_pick()
                with dve.Fori(0, E_) as e:
                    c.begin(e, (moe_link, 7), (gathered, 1), (pick_turned, 1), (silu_done_e, 14), (scattered, 2),
                            *narrow_counts(narrow))
                    for g in range(14):
                        dve.wait_ge(silu_done_e, c.up(silu_done_e))
                        TT(ex_hb[:, g % 2, :], ex_sg[:, g % 2, :], psum[:, g % 2, GU:2 * GU], ALU.mult).then_inc(hb_done_e, 1)
                        narrow_halves(2, sum(plan[:g]), plan[g])
                        if g == 12:
                            choose(e + 1)
                    lower_half()
                    for t in range(TX):
                        dve.wait_ge(scattered, c.up(scattered))
                        for n in range(2):
                            link(TT(y_acc[:, t, n * 512:(n + 1) * 512], y_acc[:, t, n * 512:(n + 1) * 512],
                                    psum[:, (6, 2)[t] + n, :], ALU.add), moe_link)
                    copy_pick()
                    c.end(E_)

            for first in (narrow_used, narrow_summed):
                c.up(first)
            dve.wait_ge(pool_cleared, 1)
            dve.wait_ge(packs_turned, c.up(packs_turned))
            dve.tensor_copy(cols[:, :], psum[:, 6, 0:310])
            dve.tensor_copy(conv_cols[:, :, :].rearrange("p c k -> p (c k)"), psum[:, 7, 0:2 * CC * TAPS]).then_inc(cols_ready, 1)
            dve.wait_ge(cols_ready, c.up(cols_ready))
            mods_to_columns(0)
            dve.wait_ge(late_in, LATE)
            for t in range(TX):
                dve.tensor_scalar(st[:, 60:61], ident[:, 0:1], 0.0, None, ALU.mult).then_inc(x_ready, 1)
                dve.wait_ge(x_ready, c.up(x_ready))
            for L in stages:
                if L < 2:
                    layer_columns(L)
                    diagonal(diag1, 0, 0)
                    norm(L, 0, T_IN[L])
                    mixer1(L)
                    gated_add(w_out_done, 2)
                    diagonal(diag1 if L == 0 else diag_moe, 1, 0)
                    norm(L, 1, 2)
                    if L == 0:
                        ffn(L, 2)
                        gated_add(down_done, 2)
                    else:
                        route()
                        link(dve.memset(y_acc, 0.0), moe_link)
                        link(dve.memset(rt[:, POS + 1, :, :], 0.0), moe_link)
                        moe(0)
                        if narrow_per_pass(1):
                            narrow_bias(2)
                        over = dve.value_load(flag[0:1, 0:1], min_val=0, max_val=1)
                        with dve.If(over > 0):
                            moe(1)
                        for t in range(TX):
                            link(TT(y_acc[:, t, :], y_acc[:, t, :], gate_bc[:, 0, :], ALU.mult))
                            TT(x[:, t, :], x[:, t, :], y_acc[:, t, :], ALU.add).then_inc(x_ready, 1)
                            dve.wait_ge(x_ready, c.up(x_ready))
                    if L == LAST1:
                        inverse_dev(TX)
                        for t in range(TX):
                            STT(x[:, t, :], x[:, t, :], st[:, RS + t:RS + t + 1], final_gain, ALU.mult, ALU.mult)\
                                .then_inc(x_ready, 1)
                            dve.wait_ge(x_ready, c.up(x_ready))
                        for t in range(TX):
                            dve.tensor_scalar(st[:, 60:61], ident[:, 0:1], 0.0, None, ALU.mult).then_inc(x_ready, 1)
                            dve.wait_ge(x_ready, c.up(x_ready))
                else:
                    layer_columns(L)
                    norm(L, 0, T_IN[L])
                    mixer2(L)
                    T = T_OUT[L]
                    for s in range(T // 2):
                        diagonal(diag2, 0, s)
                    post_add(L, T)
                    diagonal(diag2, 1, 0)
                    norm(L, 1, T)
                    if T == 4:
                        diagonal(diag2, 1, 1)
                    ffn(L, T)
                    post_add(L, T)

        @block.gpsimd
        def _(pool):
            pool.memset(eps[:, :], EPS)
            for n, free in enumerate(freed + freed2):
                pool.memset(free_marks[0:1, n:n + 1], 0.0).then_inc(free, 1)
            pool.memset(ones[:, :], 1.0).then_inc(ones_set, 1)
            pool.memset(pool_bd, 0.0).then_inc(pool_cleared, 1)
            pool.memset(free_marks[0:1, 15:16], 0.0).then_inc(narrow_spread, 2)
            pool.memset(free_marks[0:1, 14:15], 0.0).then_inc(narrow_used, 1)
            pool.memset(free_marks[0:1, 13:14], 0.0).then_inc(narrow_summed, 1)
            turned, blocks = 0, 0
            for L in stages:
                M = L + 1
                turned += T_IN[L] + T_OUT[L]
                if L == 1:
                    pool.wait_ge(x_ready, XR[1])
                    pool.dma_start(router, a["router_w"][0].rearrange("(k p) e -> p k e", p=P)).then_inc(router_in, 16)
                    pool.dma_start(router_bias, a["router_b"].to_broadcast((P, E_))).then_inc(router_in, 16)
                    pool.dma_start(iota, a["k_iota"]).then_inc(router_in, 16)
                if M > max(stages):
                    continue
                if L == 1:
                    pool.wait_ge(logits, 1)
                else:
                    pool.wait_ge(xn_turned, turned)
                n = NARROW_ALL - narrow_first(M)
                with pool.Fori(0, n) as b:
                    for h, used in enumerate((narrow_used, narrow_summed)):
                        pool.wait_ge(used, b + (blocks + 1))
                        pool.dma_start(narrow_buf(M, h), ada[M][:, 4 * h:4 * h + 4,
                                                                bass.ds(b * NARROW + narrow_first(M) * NARROW, NARROW)])\
                            .then_inc(narrow_in[h], 16)
                blocks += n


def build(nc, a, out, stages=(0, 1, 2, 3)):
    program(nc, a, out, stages)


_INS = ["x", "c", "ada_w", "ada_b", "mix_norm_g", "ffn_norm_g", "w_in", "pool_w", "pool_scale", "conv_w", "conv_b",
        "conv_ln_g", "conv_ln_b", "sgu_ln_g", "sgu_ln_b", "sgu_w", "sgu_b", "w_out", "ffn_w_gate", "ffn_w_up",
        "ffn_w_down", "router_w", "router_b", "moe_w_gate", "moe_w_up", "moe_w_down", "final_norm_g", "c_2", "ctx_2",
        "c_ctx_2", "w_mod_2", "b_mod_2", "norm_g_2", "w_in_2", "w_out_2", "hg_lb_logits_2", "hg_onorm_2",
        "da_lambda_2", "da_subln_2", "w_ffn_in_2", "w_ffn_out_2"]


def kernel(**inputs):
    import concourse.bacc as bacc
    from concourse.bass_utils import run_bass_kernel_spmd

    nc = bacc.Bacc("TRN2", target_bir_lowering=False, num_devices=1)
    arrays, aps = {}, {}
    for name in _INS:
        arrays[name] = np.ascontiguousarray(inputs[name])
    arrays.update(shape_constants())
    for name, v in arrays.items():
        aps[name] = nc.dram_tensor(name, v.shape, mybir.dt.from_np(v.dtype), kind="ExternalInput").ap()
    out = nc.dram_tensor("out", (1, SEQ, D), F32, kind="ExternalOutput").ap()
    build(nc, aps, out)
    r = run_bass_kernel_spmd(nc, [arrays], core_ids=[0])
    return r.results[0]["out"]
```
